# Optimizing a Trainium2 kernel written in Bass

```python
import jax, jax.numpy as jnp
from jax import lax
import numpy as np

D_MODEL = 2048
BATCH = 1
SEQ = 512
DEPTH = 1
DEC_BATCH = 1
DEC_SEQ = 32
PAST_LEN = 256

CHUNK = 64
EPS = 1e-6
GDN_HEADS = D_MODEL // 256
GDN_DK = 128
GDN_DV = 128
GDN_QK = GDN_HEADS * GDN_DK
GDN_VW = GDN_HEADS * GDN_DV
CONV_WIDTH = 4
CONV_DIM = 2 * GDN_QK + GDN_VW
ATT_HEADS = D_MODEL // 256
ATT_HD = 128
ATT_W = ATT_HEADS * ATT_HD
BAND_PREV = 8
BAND = (BAND_PREV + 1) * CHUNK
REL_CLIP = 128
N_REL = 2 * REL_CLIP + 1
IN_DIM = CONV_DIM + GDN_VW + 2 * GDN_HEADS + 4 * ATT_W + 2 * D_MODEL

kernel_name = 'hybrid_stream_gdn_bandattn_step'

def _split_points():
    sizes = (CONV_DIM, GDN_VW, GDN_HEADS, GDN_HEADS, ATT_W, ATT_W, ATT_W, ATT_W, D_MODEL, D_MODEL)
    return [int(s) for s in np.cumsum(sizes)[:-1]]

def rms_norm(x, w):
    x32 = x.astype(jnp.float32)
    y = x32 * lax.rsqrt(jnp.mean(x32 * x32, axis=-1, keepdims=True) + EPS)
    return (y * w.astype(jnp.float32)).astype(x.dtype)

def l2_normalize(x):
    x32 = x.astype(jnp.float32)
    return x32 * lax.rsqrt(jnp.sum(x32 * x32, axis=-1, keepdims=True) + EPS)

def gated_delta_rule(q, k, v, g, beta, s0):
    Bsz, T, H, DK = q.shape
    DV = v.shape[-1]
    C = min(CHUNK, T)
    n = T // C

    def blocks(t):
        t = t.astype(jnp.float32).reshape((Bsz, n, C, H) + t.shape[3:])
        return jnp.moveaxis(t, (1, 3), (0, 2))

    q, k, v, g, beta = blocks(q), blocks(k), blocks(v), blocks(g), blocks(beta)
    G = jnp.cumsum(g, axis=-1)
    idx = jnp.arange(C)
    incl = idx[:, None] >= idx[None, :]
    strict = idx[:, None] > idx[None, :]
    diff = G[..., :, None] - G[..., None, :]
    dmat = jnp.where(incl, jnp.exp(jnp.where(incl, diff, 0.0)), 0.0)
    kb = k * beta[..., None]
    m = jnp.where(strict, jnp.einsum('nbhid,nbhjd->nbhij', kb, k) * dmat, 0.0)
    eye = jnp.eye(C, dtype=jnp.float32)
    t_inv = lax.linalg.triangular_solve(m + eye, jnp.broadcast_to(eye, m.shape),
                                        left_side=True, lower=True)
    u = jnp.einsum('nbhij,nbhjd->nbhid', t_inv, v * beta[..., None])
    w = jnp.einsum('nbhij,nbhjd->nbhid', t_inv, kb * jnp.exp(G)[..., None])
    a_intra = jnp.einsum('nbhid,nbhjd->nbhij', q, k) * dmat
    qg = q * jnp.exp(G)[..., None]
    kg = k * jnp.exp(G[..., -1:] - G)[..., None]
    g_last = jnp.exp(G[..., -1])

    def step(s, xs):
        qg_c, kg_c, u_c, w_c, a_c, gl = xs
        v_new = u_c - jnp.einsum('bhid,bhde->bhie', w_c, s)
        o = jnp.einsum('bhid,bhde->bhie', qg_c, s) + jnp.einsum('bhij,bhje->bhie', a_c, v_new)
        s = s * gl[..., None, None] + jnp.einsum('bhid,bhie->bhde', kg_c, v_new)
        return s, o

    s_fin, o = lax.scan(step, s0.astype(jnp.float32), (qg, kg, u, w, a_intra, g_last))
    o = jnp.moveaxis(o, (0, 2), (1, 3)).reshape(Bsz, T, H, DV)
    return o, s_fin

def gdn_branch(qkv, gate, b_raw, a_raw, conv_buf, s0, conv_w, a_log, dt_bias, norm_w):
    Bsz, T, _ = qkv.shape
    full = jnp.concatenate([conv_buf.astype(qkv.dtype), qkv], axis=1)
    conv = full[:, 0:T] * conv_w[0]
    for i in range(1, CONV_WIDTH):
        conv = conv + full[:, i:i + T] * conv_w[i]
    new_buf = full[:, full.shape[1] - (CONV_WIDTH - 1):]
    act = jax.nn.silu(conv)
    q, k, v = jnp.split(act, [GDN_QK, 2 * GDN_QK], axis=-1)
    q = l2_normalize(q.reshape(Bsz, T, GDN_HEADS, GDN_DK)) * (GDN_DK ** -0.5)
    k = l2_normalize(k.reshape(Bsz, T, GDN_HEADS, GDN_DK))
    v = v.reshape(Bsz, T, GDN_HEADS, GDN_DV)
    beta = jax.nn.sigmoid(b_raw.astype(jnp.float32))
    g = -jnp.exp(a_log.astype(jnp.float32)) * jax.nn.softplus(
        a_raw.astype(jnp.float32) + dt_bias.astype(jnp.float32))
    o, s_new = gated_delta_rule(q, k, v, g, beta, s0)
    o = rms_norm(o, norm_w).reshape(Bsz, T, GDN_VW).astype(qkv.dtype) * jax.nn.silu(gate)
    return o, new_buf, s_new.astype(s0.dtype)

def band_attention(q, k, v, q_pos, k_pos, rel_bias):
    s = jnp.einsum('bqhd,bkhd->bhqk', q, k).astype(jnp.float32) * (ATT_HD ** -0.5)
    dist = jnp.clip(q_pos[:, None] - k_pos[None, :], -REL_CLIP, REL_CLIP) + REL_CLIP
    s = s + rel_bias[:, dist].astype(jnp.float32)[None]
    qc = q_pos // CHUNK
    kc = k_pos // CHUNK
    valid = (k_pos[None, :] >= 0) & (kc[None, :] <= qc[:, None]) & (kc[None, :] >= qc[:, None] - BAND_PREV)
    s = jnp.where(valid[None, None], s, -1e30)
    p = jax.nn.softmax(s, axis=-1)
    return jnp.einsum('bhqk,bkhd->bqhd', p.astype(v.dtype), v)

def band_attention_prompt(q, k, v, rel_bias):
    Bsz, T, H, D = q.shape
    pad = BAND_PREV * CHUNK
    k_pad = jnp.pad(k, ((0, 0), (pad, 0), (0, 0), (0, 0)))
    v_pad = jnp.pad(v, ((0, 0), (pad, 0), (0, 0), (0, 0)))

    def one_chunk(ci):
        start = ci * CHUNK
        q_c = lax.dynamic_slice_in_dim(q, start, CHUNK, axis=1)
        k_c = lax.dynamic_slice_in_dim(k_pad, start, BAND, axis=1)
        v_c = lax.dynamic_slice_in_dim(v_pad, start, BAND, axis=1)
        q_pos = start + jnp.arange(CHUNK)
        k_pos = start - pad + jnp.arange(BAND)
        return band_attention(q_c, k_c, v_c, q_pos, k_pos, rel_bias)

    o = lax.map(one_chunk, jnp.arange(T // CHUNK))
    return jnp.moveaxis(o, 0, 1).reshape(Bsz, T, H, D)

def layer(x, c, conv_buf, s0, k_cache, v_cache, p, prompt):
    (norm_w, ada_w, ada_b, w_in, conv_w, a_log, dt_bias, gdn_norm_w,
     q_norm_w, k_norm_w, rel_bias, w_proj_a, w_proj_b, w_out) = p
    Bsz, T, _ = x.shape
    mod = jax.nn.silu(c) @ ada_w + ada_b
    shift, scale, gate = jnp.split(mod, 3, axis=-1)
    h = rms_norm(x, norm_w) * (1 + scale[:, None, :]) + shift[:, None, :]
    z = h @ w_in
    (qkv_a, gate_a, b_a, a_a, q_b, k_b, v_b, gate_b, m_a, m_b) = jnp.split(z, _split_points(), axis=-1)
    o_a, new_buf, s_new = gdn_branch(qkv_a, gate_a, b_a, a_a, conv_buf, s0, conv_w,
                                     a_log, dt_bias, gdn_norm_w)
    q = rms_norm(q_b.reshape(Bsz, T, ATT_HEADS, ATT_HD), q_norm_w)
    k = rms_norm(k_b.reshape(Bsz, T, ATT_HEADS, ATT_HD), k_norm_w)
    v = v_b.reshape(Bsz, T, ATT_HEADS, ATT_HD)
    if prompt:
        o_b = band_attention_prompt(q, k, v, rel_bias)
        keep = min(BAND_PREV * CHUNK, T)
        k_new = k[:, T - keep:]
        v_new = v[:, T - keep:]
    else:
        n_cached = k_cache.shape[1]
        k_all = jnp.concatenate([k_cache.astype(k.dtype), k], axis=1)
        v_all = jnp.concatenate([v_cache.astype(v.dtype), v], axis=1)
        q_pos = PAST_LEN + jnp.arange(T)
        k_pos = PAST_LEN - n_cached + jnp.arange(n_cached + T)
        o_b = band_attention(q, k_all, v_all, q_pos, k_pos, rel_bias)
        k_new = k
        v_new = v
    o_b = o_b.reshape(Bsz, T, ATT_W) * jax.nn.silu(gate_b)
    merged = jax.nn.sigmoid(m_a) * (o_a @ w_proj_a) + jax.nn.sigmoid(m_b) * (o_b @ w_proj_b)
    y = x + gate[:, None, :] * (merged @ w_out)
    return y, new_buf, s_new, k_new, v_new

def setup_inputs(seed: int = 0) -> dict:
    key = jax.random.key(seed)
    ks = jax.random.split(key, 24)
    f32 = jnp.float32
    n_cached = min(BAND_PREV * CHUNK, PAST_LEN)
    nrm = lambda k, shape, s: jax.random.normal(k, shape, f32) * s
    dt = jnp.exp(jax.random.uniform(ks[12], (DEPTH, GDN_HEADS), f32, np.log(1e-3), np.log(1e-1)))
    return {
        'x_prompt': nrm(ks[0], (BATCH, SEQ, D_MODEL), 1.0),
        'x_sample': nrm(ks[1], (DEC_BATCH, DEC_SEQ, D_MODEL), 1.0),
        'c_prompt': nrm(ks[2], (BATCH, D_MODEL), 1.0),
        'c_sample': nrm(ks[3], (DEC_BATCH, D_MODEL), 1.0),
        'state_conv': nrm(ks[4], (DEPTH, DEC_BATCH, CONV_WIDTH - 1, CONV_DIM), 1.0),
        'state_delta': nrm(ks[5], (DEPTH, DEC_BATCH, GDN_HEADS, GDN_DK, GDN_DV), 0.1),
        'cache_k': nrm(ks[6], (DEPTH, DEC_BATCH, n_cached, ATT_HEADS, ATT_HD), 1.0),
        'cache_v': nrm(ks[7], (DEPTH, DEC_BATCH, n_cached, ATT_HEADS, ATT_HD), 1.0),
        'norm_w': 1.0 + nrm(ks[8], (DEPTH, D_MODEL), 0.02),
        'ada_w': nrm(ks[9], (DEPTH, D_MODEL, 3 * D_MODEL), 0.5 * D_MODEL ** -0.5),
        'ada_b': nrm(ks[10], (DEPTH, 3 * D_MODEL), 0.02),
        'w_in': nrm(ks[11], (DEPTH, D_MODEL, IN_DIM), D_MODEL ** -0.5),
        'conv_w': nrm(ks[13], (DEPTH, CONV_WIDTH, CONV_DIM), 0.5),
        'gdn_a_log': jnp.log(jax.random.uniform(ks[14], (DEPTH, GDN_HEADS), f32, 1.0, 16.0)),
        'gdn_dt_bias': dt + jnp.log(-jnp.expm1(-dt)),
        'gdn_norm_w': 1.0 + nrm(ks[15], (DEPTH, GDN_DV), 0.02),
        'q_norm_w': 1.0 + nrm(ks[16], (DEPTH, ATT_HD), 0.02),
        'k_norm_w': 1.0 + nrm(ks[17], (DEPTH, ATT_HD), 0.02),
        'rel_bias': nrm(ks[18], (DEPTH, ATT_HEADS, N_REL), 0.3),
        'w_proj_a': nrm(ks[19], (DEPTH, GDN_VW, D_MODEL), GDN_VW ** -0.5),
        'w_proj_b': nrm(ks[20], (DEPTH, ATT_W, D_MODEL), ATT_W ** -0.5),
        'w_out': nrm(ks[21], (DEPTH, D_MODEL, D_MODEL), D_MODEL ** -0.5),
    }

def reference(x_prompt, x_sample, c_prompt, c_sample, state_conv, state_delta, cache_k, cache_v,
              norm_w, ada_w, ada_b, w_in, conv_w, gdn_a_log, gdn_dt_bias, gdn_norm_w,
              q_norm_w, k_norm_w, rel_bias, w_proj_a, w_proj_b, w_out):
    yp = x_prompt
    ys = x_sample
    p_conv, p_delta, p_k, p_v = [], [], [], []
    s_conv, s_delta, s_k, s_v = [], [], [], []
    Bp = x_prompt.shape[0]
    for l in range(DEPTH):
        params = (norm_w[l], ada_w[l], ada_b[l], w_in[l], conv_w[l], gdn_a_log[l], gdn_dt_bias[l],
                  gdn_norm_w[l], q_norm_w[l], k_norm_w[l], rel_bias[l], w_proj_a[l], w_proj_b[l], w_out[l])
        zero_buf = jnp.zeros((Bp, CONV_WIDTH - 1, CONV_DIM), x_prompt.dtype)
        zero_state = jnp.zeros((Bp, GDN_HEADS, GDN_DK, GDN_DV), state_delta.dtype)
        yp, cb, sd, kk, vv = layer(yp, c_prompt, zero_buf, zero_state, None, None, params, True)
        p_conv.append(cb); p_delta.append(sd); p_k.append(kk); p_v.append(vv)
        ys, cb, sd, kk, vv = layer(ys, c_sample, state_conv[l], state_delta[l], cache_k[l], cache_v[l],
                                   params, False)
        s_conv.append(cb); s_delta.append(sd); s_k.append(kk); s_v.append(vv)
    return (yp, ys,
            jnp.stack(p_conv), jnp.stack(p_delta), jnp.stack(p_k), jnp.stack(p_v),
            jnp.stack(s_conv), jnp.stack(s_delta), jnp.stack(s_k), jnp.stack(s_v))


_drawn_inputs = setup_inputs


def setup_inputs(seed=0):
    import zlib

    import numpy as np

    out = dict(_drawn_inputs(seed))
    spreads = {}
    factors = {'cache_k': 7.454,
     'cache_v': 5.854,
     'gdn_norm_w': 8.0,
     'q_norm_w': 8.0,
     'k_norm_w': 2.886,
     'rel_bias': 8.0}
    for name, (base, spread) in spreads.items():
        noise = np.random.default_rng([zlib.crc32(name.encode()), seed]).standard_normal(out[name].shape)
        drawn = base * np.exp(spread * noise) if base else spread * noise
        out[name] = __import__('jax').numpy.asarray(drawn.astype(out[name].dtype))
    for name, factor in factors.items():
        out[name] = (out[name] * factor).astype(out[name].dtype)
    return out
```

```python
from contextlib import ExitStack

import numpy as np

import concourse.bass as bass
from concourse import mybir

F32 = mybir.dt.float32
F32R = mybir.dt.float32r
ACT = mybir.ActivationFunctionType
ALU = mybir.AluOpType
AX = mybir.AxisListType

P = 128
D = 2048
NP = 512
NS = 32
N = NP + NS
HALF = N // 2
KT = D // P
HEADS = 8
NT = NP // P
CH = 64
NCH = NP // CH
EPS = 1e-6
QK = HEADS * P
COL_BA = 4 * QK
COL_B = COL_BA + 2 * HEADS
COL_M = COL_B + 4 * QK
IN_DIM = COL_M + 2 * D
RING = 4
SLOT = 512
LEAD = 2
GRID = 64
PAST = 256
MASKED = -1e30
INV = 184
EXP_LN_SET = 6

IDENT, UPPER, BLOCK, STRICT, PAIR_T, PAIR, LEVEL2 = 0, 1, 2, 3, 4, 5, 6
LEVELS = (2, 3, 4, 5, 6)
ROWS_A, ROWS_B = LEVEL2 + len(LEVELS), LEVEL2 + len(LEVELS) + 1
NCONST = ROWS_B + 1


def constants():
    i = np.arange(P)
    r, c = i[:, None], i[None, :]
    same = (r // CH) == (c // CH)
    out = np.zeros((NCONST, P, P), np.float32)
    out[IDENT] = r == c
    out[UPPER] = same & (r <= c)
    out[BLOCK] = same
    out[STRICT] = same & (r < c)
    out[PAIR] = -1.0 * ((r // 2 == c // 2) & (r > c))
    out[PAIR_T] = out[PAIR].T
    for n, level in enumerate(LEVELS):
        size = 2 ** level
        out[LEVEL2 + n] = (r // size == c // size) & (r // (size // 2) != c // (size // 2)) & (r > c)
    out[ROWS_A] = (r < CH) & (c >= 0)
    out[ROWS_B] = (r >= CH) & (c >= 0)
    return np.ascontiguousarray(out.transpose(1, 0, 2))


SEMAPHORES = """
c_load x_load0 x_load1 wba_load row_load vec_ps vec_sb cT_ps cT_e cT x_ss x_e x_n xt_ps xt ada_row ada_cps ada_col
h_full h_hi h_lo wba_hi wba_lo ba_ps ba_sb g_e1 g_e2 g_e3 g_g cum_ps cum_sb cum_d gates zeroed
ada_used hi lo used act_link dve_link pool_link
cin_ready conv_done exp_a act_ready bss tails nat_ps nat_a sq_a ss_a x_a y_a scal_a knb_a pool_a gbc tr_a tra_act tra_dve
grow_ps diff et em mt_ps mt at_ps at m_ps m bm st0 lx_ps lx ly_ps ly lt_ps lt w_ps w_sb u_ps u_sb
sa_ps vn sb_ps so ss_new s_load s_zero s_out sq_o x_o y_o on_o o_ps oa ga_z ga_e sga
bz bnat_ps bnat bsq x_b y_b bk_y bkw bqn cache_load ct_ps ct bias_load bias btr_ps btr
qk sadd smax pexp pn pt_ps pt pv ob gb_z gb_e sgb k_out v_out cs_ps cs_sb cs_out
o_hi o_lo m_e m_sig mrg_a mrg m_hi m_lo f_g f_ps f_sb x_tail0 x_tail1 y_out0 y_out1
""".split()


class Link:

    def __init__(self, eng, sem):
        self.eng, self.sem, self.n, self.extra, self.start = eng, sem, 0, 0, 0

    def __call__(self, ins):
        self.n += 1
        ins.then_inc(self.sem, 1)
        self.eng.wait_ge(self.sem, self.n + self.extra)

    def loop(self, i, first, per):
        self.start, self.extra, self.per = self.n, (i - first) * per, per

    def end(self, times):
        assert self.n - self.start == self.per, (self.n - self.start, self.per)
        self.n, self.extra = self.start + self.per * times, 0


def again(h):
    return not (isinstance(h, int) and h == 0)


def hybrid_layer(nc, io):
    ctx = ExitStack()
    with ctx:
        def sb(name, shape, dt=F32, where=ctx):
            return where.enter_context(nc.sbuf_tensor(name, shape, dt))

        s = {n: ctx.enter_context(nc.semaphore(n)) for n in SEMAPHORES}
        x_tail = [s["x_tail0"], s["x_tail1"]]
        y_out = [s["y_out0"], s["y_out1"]]
        landed = [ctx.enter_context(nc.semaphore(f"landed{r}")) for r in range(RING)]

        ps = ctx.enter_context(nc.psum_tensor("ps", [P, 8, 512], F32))
        G1, G2, A1, A2 = 4, 5, 6, 7

        Hh = sb("Hh", [P, KT, N], F32R)
        Hl = sb("Hl", [P, KT, N], F32R)
        Of = sb("Of", [P, KT, N])
        raw = sb("raw", [P, RING, SLOT])
        whi = sb("whi", [P, RING, SLOT], F32R)
        wlo = sb("wlo", [P, RING, SLOT], F32R)
        eye = sb("eye", [P, P])
        modT = sb("modT", [P, 3 * KT, 2])
        vecT = sb("vecT", [P, 2, P])
        cv = sb("cv", [P, KT, 2])
        cvs = sb("cvs", [P, KT, 2])
        conv_cols = vecT[:, 0, 0:96].rearrange("p (i b) -> p b i", i=4)
        norm_col = vecT[:, 0, 96:112]
        gnw_col = vecT[:, 0, 112:113]
        qnw_col = vecT[:, 0, 113:114]
        state_cols = vecT[:, 1, 0:72].rearrange("p (i b) -> p b i", i=3)
        adab_cols = vecT[:, 1, 72:120]

        NG = HEADS * (NT + 1)
        gsz = [P, HEADS, NT + 1]
        beta, gg, Gc, eG, egl = (sb(n, gsz) for n in ("beta", "gg", "Gc", "eG", "egl"))
        glb = sb("glb", [P, 2, HEADS, NT + 1])
        cs = sb("cs", [P, 6, 24])

        masks = ExitStack()
        con = sb("con", [P, NCONST, P], where=masks)

        begin = ExitStack()
        xT = sb("xT", [P, KT, N], where=begin)
        xn = [sb(f"xn{i}", [P, D], where=begin) for i in range(2)]
        junk = sb("junk", [P, D], where=begin)
        mrow = sb("mrow", [2, SLOT], where=begin)
        vrow = sb("vrow", [P, 2, P], where=begin)
        crow = sb("crow", [2 * KT, P], where=begin)
        ce = sb("ce", [P, 2 * KT], where=begin)
        xs = sb("xs", [P, 8], where=begin)
        hA = sb("hA", [P, KT, 2], where=begin)
        wba = sb("wba", [P, KT, 16], where=begin)
        wbs = sb("wbs", [P, KT, 2, 16], F32R, where=begin)
        bar = sb("bar", [P, NT + 1, 32], where=begin)
        bax = sb("bax", [P, 2 * HEADS, NT + 1], where=begin)
        dtb = sb("dtb", [P, 2, HEADS], where=begin)
        gt = [sb(f"gt{i}", gsz, where=begin) for i in range(6)]
        begin.close()

        heads = ExitStack()
        def nat(name):
            return sb(name, [P, NT + 1, P], where=heads)
        cin = sb("cin", [P, 3 + N + 3], where=heads)
        cacc = sb("cacc", [P, N + 3], where=heads)
        eT = sb("eT", [P, N + 3], where=heads)
        aT = sb("aT", [P, N], where=heads)
        q_nat, k_nat, v_nat, sqb, Mn, B0, B1, MT, AT, Sm, Tm, Xs, vb, kbg, kg = (nat(n) for n in (
            "q_nat", "k_nat", "v_nat", "sqb", "Mn", "B0", "B1", "MT", "AT", "Sm", "Tm", "Xs", "vb", "kbg", "kg"))
        kn, kb, qn, qg, U_, o_nat, ET, EU, ES, gbc = Mn, B0, B1, MT, MT, v_nat, sqb, Sm, Tm, Xs
        knT = sb("knT", [P, N], where=heads)
        kbT = sb("kbT", [P, N], where=heads)
        qnT = sb("qnT", [P, N], where=heads)
        qgw = sb("qgw", [P, (NCH + 1) * P], where=heads)
        Vn = sb("Vn", [P, P], where=heads)
        Vs = sb("Vs", [NS, P], where=heads)
        St = sb("St", [P, P], where=heads)
        Ss = sb("Ss", [P, P], where=heads)
        sga = sb("sga", [P, N], where=heads)
        sgb = sb("sgb", [P, N], where=heads)
        bv = nat("bv")
        kc = sb("kc", [P, 2, P], where=heads)
        vc = sb("vc", [P, 2, P], where=heads)
        kcT = sb("kcT", [P, PAST], where=heads)
        Bp = sb("Bp", [P, 2 * P], where=heads)
        kwb = sb("kwb", [P, P], where=heads)
        st = sb("st", [P, 16, 5], where=heads)
        sm = sb("sm", [P, 2, 4], where=heads)
        heads.close()
        bq, bk = q_nat, k_nat
        kT, qT, PT = knT, qnT, kbT
        Pb = [Xs, B0]
        csT = cacc[:, 0:2 * P].rearrange("p (a n) -> p a n", a=2)
        mrows = [mrow, eT[0:2, 0:SLOT]]
        (SS_Q, SS_K, X_Q, X_K, Y_Q, Y_K, T_Q, T_K, SC_Q, SC_QG, SC_KB, SC_KBG, SC_KG) = range(13)

        masks.close()
        late = ExitStack()
        Oh = sb("Oh", [P, KT, N], F32R, where=late)
        Ol = sb("Ol", [P, KT, N], F32R, where=late)
        sg = [sb(f"sg{i}", [P, N], where=late) for i in range(2)]
        tmp = sb("tmp", [P, N], where=late)
        late.close()
        last = ExitStack()
        fo = sb("fo", [P, 2, N], where=last)
        xr = sb("xr", [P, 2, NT + 1, P], where=last)
        yo = sb("yo", [P, 2, NT + 1, P], where=last)
        last.close()

        w_in = io["w_in"].rearrange("o d n -> (o d) n")
        ada_w = io["ada_w"].rearrange("o d n -> (o d) n")
        wpa = io["w_proj_a"].rearrange("o d n -> (o d) n")
        wpb = io["w_proj_b"].rearrange("o d n -> (o d) n")
        w_out = io["w_out"].rearrange("o d n -> (o d) n")
        x_p = io["x_prompt"].rearrange("b t d -> (b t) d")
        x_s = io["x_sample"].rearrange("b t d -> (b t) d")
        y_p = io["y_prompt"].rearrange("b t d -> (b t) d")
        y_s = io["y_sample"].rearrange("b t d -> (b t) d")
        sdelta = io["state_delta"].rearrange("o b h k v -> (o b h) k v")
        pdel_o = io["p_delta"].rearrange("o b h k v -> (o b h) k v")
        sdel_o = io["s_delta"].rearrange("o b h k v -> (o b h) k v")
        ck = io["cache_k"].rearrange("o b t h d -> h (o b t) d")
        cvd = io["cache_v"].rearrange("o b t h d -> h (o b t) d")
        kv_o = {n: io[n].rearrange("o b t h d -> h (o b t) d") for n in ("p_k", "p_v", "s_k", "s_v")}
        relx = io["rel_ext"]

        def blocks_of(w, row0, col0, count=4):
            return w[row0:row0 + count * P, bass.ds(col0, P)].rearrange("(a p) n -> p a n", p=P)

        def split4(ap):
            return ap.rearrange("p (a n) -> p a n", a=4)

        def bank(b, cols=512):
            return ps[:, b, 0:cols]

        def tiles(b):
            return ps[:, b, :].rearrange("p (t n) -> p t n", t=4)

        def acc(pair):
            return ps[:, 2 * pair:2 * pair + 2, 0:HALF]

        def halves(ap):
            return ap.rearrange("p (a n) -> p a n", a=2)

        def wide(cols):
            return cols.unsqueeze(2).to_broadcast([cols.shape[0], cols.shape[1], P])

        block = ctx.enter_context(nc.Block())

        SL_MERGE = 32 * HEADS
        SL_OUT = SL_MERGE + 12 * KT
        ADA = 128
        ADA_GATE = 64

        @block.sync
        def _(sp):
            def ada_slot(c, k, col):
                r = k % RING
                if not (isinstance(c, int) and c == 0 and k < RING):
                    sp.wait_ge(s["ada_used"], 16 * c + k - RING + 1)
                sp.dma_start(raw[:, r, :], ada_w[k * P:(k + 1) * P, bass.ds(col, SLOT)]).then_inc(landed[r], 16)

            def slot(n, r, src):
                sp.wait_ge(s["lo"], n - RING + 1)
                sp.dma_start(split4(raw[:, r, :]), src).then_inc(landed[r], 16)

            for c in range(2):
                for k in range(KT):
                    ada_slot(c, k, D * (1 - c))
            with sp.Fori(0, 3) as i:
                for half in range(2):
                    for k in range(KT):
                        ada_slot(i * 2 + 2 + half, k, i * SLOT + (SLOT + D * (1 - half)))

            unit_cols = [0, QK, 2 * QK, 3 * QK, COL_B, COL_B + QK, COL_B + 2 * QK, COL_B + 3 * QK]

            def head_slots(h, first):
                for u, col in enumerate(unit_cols):
                    for k4 in range(4):
                        c = 4 * u + k4
                        if first and c < RING:
                            sp.wait_ge(s["ada_used"], ADA - RING + c + 1)
                            sp.dma_start(split4(raw[:, c, :]), blocks_of(w_in, 512 * k4, h * P + col)).then_inc(landed[c], 16)
                        else:
                            slot(h * 32 + c, c % RING, blocks_of(w_in, 512 * k4, h * P + col))

            head_slots(0, True)
            with sp.Fori(1, HEADS) as h:
                head_slots(h, False)
            for c in range(ADA_GATE // KT):
                for k in range(KT):
                    g = KT * c + k
                    if g < RING:
                        sp.wait_ge(s["lo"], SL_MERGE - RING + g + 1)
                    else:
                        sp.wait_ge(s["ada_used"], ADA + g - RING + 1)
                    sp.dma_start(raw[:, k % RING, :], ada_w[k * P:(k + 1) * P, 2 * D + c * SLOT:2 * D + (c + 1) * SLOT]).then_inc(landed[k % RING], 16)

            def merge_slots(i, first):
                for c in range(12):
                    if c < 8:
                        src = blocks_of(w_in, 512 * (c % 4), i * P + (first * P + COL_M + D * (c // 4)))
                    else:
                        src = blocks_of(wpa if c < 10 else wpb, 512 * (c % 2), i * P + first * P)
                    if first or c >= RING:
                        slot(i * 12 + (12 * first + SL_MERGE + c), c % RING, src)
                    else:
                        sp.wait_ge(s["ada_used"], ADA + ADA_GATE - RING + c + 1)
                        sp.dma_start(split4(raw[:, c, :]), src).then_inc(landed[c], 16)
            merge_slots(0, 0)
            with sp.Fori(0, KT - 1) as i:
                merge_slots(i, 1)
            with sp.Fori(0, KT) as j:
                for c in range(4):
                    slot(j * 4 + SL_OUT + c, c, blocks_of(w_out, 512 * c, j * P))

        def split_hi(act, base, c, ada=ADA):
            r = c % RING
            act.wait_ge(landed[r], (base + (c - r)) * (16 // RING) + 16 * (ada // RING + 1))
            if not (isinstance(base, int) and base + c < RING):
                act.wait_ge(s["used"], base + (c - RING + 1))
            act.activation(whi[:, r, :], raw[:, r, :], ACT.Copy).then_inc(s["hi"], 1)

        def split_lo(dve, base, c):
            r = c % RING
            dve.wait_ge(s["hi"], base + (c + 1))
            dve.tensor_tensor(wlo[:, r, :], raw[:, r, :], whi[:, r, :].bitcast(F32), ALU.subtract).then_inc(s["lo"], 1)

        def rsqrt_newton(link, dve, y, x, t):
            link(dve.tensor_tensor(t, y, y, ALU.mult))
            link(dve.tensor_tensor(t, t, x, ALU.mult))
            link(dve.tensor_scalar(t, t, -0.5, 1.5, ALU.mult, ALU.add))
            link(dve.tensor_tensor(y, y, t, ALU.mult))

        def run_head(steps, h, place):
            for at, step in steps:
                if at == place + GRID and again(h):
                    step(h - 1)
            for at, step in steps:
                if at == place:
                    step(h)

        def run_tail(steps, place):
            for at, step in steps:
                if at == place + GRID:
                    step(HEADS - 1)

        @block.scalar
        def _(act):
            link = Link(act, s["act_link"])
            act.add_instruction(mybir.InstLoadActFuncSet(name=nc.get_next_instruction_name(), act_func_set_id=EXP_LN_SET, engine=mybir.EngineType.Activation))

            def a_evac(i):
                def go(h):
                    pair = i % 2
                    act.wait_ge(s["used"], h * 32 + 4 * (i + 1))
                    if not again(h):
                        act.wait_ge(s["zeroed"], 1)
                    if i or again(h):
                        act.wait_ge(s["conv_done"], h * 3 + i)
                        act.wait_ge(s["tails"], h * 3 + i)
                    act.copy(cin[:, 3:3 + HALF], ps[:, 2 * pair, 0:HALF])
                    act.copy(cin[:, 3 + HALF:3 + NP], ps[:, 2 * pair + 1, 0:NP - HALF])
                    act.copy(cin[:, 6 + NP:6 + N], ps[:, 2 * pair + 1, NP - HALF:HALF])
                    act.copy(cin[:, 3 + NP:6 + NP], state_cols[:, h + 8 * i, :]).then_inc(s["cin_ready"], 1)
                return go

            def a_exp(i):
                def go(h):
                    act.wait_ge(s["conv_done"], h * 3 + i + 1)
                    if i == 0 and again(h):
                        act.wait_ge(s["sgb"], h)
                    act.activation(eT[:, :], cacc[:, :], ACT.Exp, scale=-1.0).then_inc(s["exp_a"], 1)
                return go

            def evac_nat(ps_sem, sb_sem, dst, count, bank_a):
                def go(h):
                    act.wait_ge(s[ps_sem], h * 3 + count)
                    act.copy(dst[:, 0:NT, :], tiles(bank_a))
                    act.copy(dst[0:NS, NT, :], ps[0:NS, bank_a + 1, 0:P]).then_inc(s[sb_sem], 1)
                return go

            def a_nat(i):
                def go(h):
                    if again(h) and i < 2:
                        act.wait_ge(s["bqn" if i == 0 else "btr_ps"], h if i == 0 else 2 * h)
                        act.wait_ge(s["bnat_ps"], 3 * h)
                        if i == 1:
                            act.wait_ge(s["k_out"], 32 * h)
                    if again(h) and i == 2:
                        act.wait_ge(s["o_ps"], h)
                    evac_nat("nat_ps", "nat_a", (q_nat, k_nat, v_nat)[i], i + 1, G1 if i < 2 else A1)(h)
                return go

            def a_lnexp(x_sem, y_sem, lo, n):
                def go(h):
                    act.wait_ge(s[x_sem], h + 1)
                    link(act.activation(st[:, T_Q:T_Q + n, :], st[:, X_Q:X_Q + n, :], ACT.Ln))
                    act.activation(st[:, Y_Q:Y_Q + n, :], st[:, T_Q:T_Q + n, :], ACT.Exp, scale=-0.5).then_inc(s[y_sem], 1)
                return go

            def a_trev(dst, n):
                def go(h):
                    act.wait_ge(s["tr_a"], h * 4 + (1, 3, 4)[n])
                    if n < 2:
                        act.copy(dst[:, 0:NP], bank(G1))
                        act.copy(dst[:, NP:N], ps[:, G2, 0:NS]).then_inc(s["tra_act"], 1)
                    else:
                        act.copy(qgw[:, CH:CH + 4 * 256].rearrange("p (t n) -> p t n", n=256)[:, :, 0:P], tiles(G1))
                        act.copy(qgw[:, NCH * P + NS:NCH * P + 2 * NS], ps[:, G2, 0:NS]).then_inc(s["tra_act"], 1)
                return go

            def a_et(h):
                act.wait_ge(s["diff"], h + 1)
                act.activation(ET[:, 0:NT, :], ET[:, 0:NT, :], ACT.Exp)
                act.activation(ET[0:NS, NT, 0:NS], ET[0:NS, NT, 0:NS], ACT.Exp).then_inc(s["et"], 1)

            def a_m(h):
                act.wait_ge(s["m_ps"], h + 1)
                act.copy(Mn[:, 0:NT, :], tiles(G1))
                act.copy(Mn[0:NS, NT, 0:NS], ps[0:NS, G2, 0:NS]).then_inc(s["m"], 1)

            def level_evac(ps_sem, sb_sem, dst, per, n):
                def go(h):
                    act.wait_ge(s[ps_sem], h * per + n + 1)
                    act.copy(dst[:, 0:NT, :], tiles(G1))
                    act.copy(dst[0:NS, NT, 0:NS], ps[0:NS, G2, 0:NS]).then_inc(s[sb_sem], 1)
                return go

            def a_w(h):
                act.wait_ge(s["w_ps"], h + 1)
                for a in range(2):
                    act.copy(qgw[:, 0:NCH * P].rearrange("p (t n) -> p t n", n=256)[:, :, 192 * a:192 * a + CH],
                             tiles(G1)[:, :, CH * a:CH * a + CH])
                act.copy(qgw[:, NCH * P:NCH * P + NS], ps[:, G2, 0:NS]).then_inc(s["w_sb"], 1)

            def a_o(n):
                def go(h):
                    act.wait_ge(s["sb_ps"], h * 9 + max(n, 1) + 1)
                    if n == 0:
                        ins = act.copy(o_nat[0:NS, NT, :], ps[NS:2 * NS, G1, P:2 * P])
                    else:
                        c = n - 1
                        r0 = CH * (c % 2)
                        ins = act.copy(o_nat[r0:r0 + CH, c // 2, :], ps[CH - r0:2 * CH - r0, G1, 0:P])
                    ins.then_inc(s["so"], 1)
                return go

            def gate_evac(u, z, sem):
                def go(h):
                    act.wait_ge(s["used"], h * 32 + 4 * (u + 1))
                    if again(h):
                        act.wait_ge(s["oa" if u == 3 else "ob"], h if u == 3 else 5 * h)
                    act.copy(halves(z[:, :]), acc(1)).then_inc(s[sem], 1)
                return go

            def gate_exp(z, z_sem, sem):
                def go(h):
                    act.wait_ge(s[z_sem], h + 1)
                    if z is sga:
                        act.wait_ge(s["act_ready"], h * 3 + 3)
                    else:
                        act.wait_ge(s["sga"], h + 1)
                    act.activation(eT[:, 0:N], z[:, :], ACT.Exp, scale=-1.0).then_inc(s[sem], 1)
                return go

            def b_evac(i):
                def go(h):
                    pair = i % 2
                    act.wait_ge(s["used"], h * 32 + 4 * (5 + i))
                    if i == 0:
                        act.wait_ge(s["nat_ps"], h * 3 + 3)
                    else:
                        act.wait_ge(s["bnat_ps"], h * 3 + i)
                    act.copy(halves(aT[:, :]), acc(pair)).then_inc(s["bz"], 1)
                return go

            def b_nat(i):
                def go(h):
                    if i == 0:
                        act.wait_ge(s["pool_a"], h * 5 + 2)
                    if i == 1:
                        act.wait_ge(s["pool_a"], h * 5 + 5)
                    if i == 2 and again(h):
                        act.wait_ge(s["pv"], 5 * h)
                        act.wait_ge(s["v_out"], 32 * h)
                    evac_nat("bnat_ps", "bnat", (bq, bk, bv)[i], i + 1, A1)(h)
                return go

            def b_ct(h):
                act.wait_ge(s["ct_ps"], h + 1)
                act.copy(kcT[:, :], ps[:, A1, 0:PAST]).then_inc(s["ct"], 1)

            def b_trev(n):
                def go(h):
                    act.wait_ge(s["btr_ps"], h * 2 + n + 1)
                    act.wait_ge(s["at_ps"], h + 1)
                    dst = (kT, qT)[n]
                    if n == 0:
                        act.copy(dst[:, 0:NP], bank(A1))
                        act.copy(dst[:, NP:N], ps[:, A2, 0:NS]).then_inc(s["btr"], 1)
                    else:
                        act.activation(dst[:, 0:NP], bank(A1), ACT.Copy, scale=qnw_col)
                        act.activation(dst[:, NP:N], ps[:, A2, 0:NS], ACT.Copy, scale=qnw_col).then_inc(s["btr"], 1)
                return go

            def key_count(i):
                return (i + 1) * P if i < NT else PAST + NS

            def b_exp(i):
                def go(h):
                    rows = P if i < NT else NS
                    n = key_count(i)
                    act.wait_ge(s["smax"], h * 5 + i + 1)
                    p = Pb[i % 2][0:rows, :, :].rearrange("p a n -> p (a n)")[:, 0:n]
                    act.activation(p, p, ACT.Exp, bias=sm[0:rows, i % 2, 0:1], accum_out=sm[0:rows, i % 2, 1:2]).then_inc(s["pexp"], 1)
                return go

            def b_pt(i):
                def go(h):
                    act.wait_ge(s["pt_ps"], h * 5 + i + 1)
                    if i == 0:
                        act.wait_ge(s["mt_ps"], h + 1)
                    else:
                        act.wait_ge(s["pv"], h * 5 + i)
                    if i < NT:
                        n = (i + 1) * P
                        act.copy(PT[:, 0:n], ps[:, A2, 0:n]).then_inc(s["pt"], 1)
                    else:
                        act.copy(PT[:, 0:2 * NS], ps[:, A2, 0:2 * NS])
                        act.copy(PT[0:NS, 2 * NS:3 * NS], ps[0:NS, A2, 2 * NS:3 * NS]).then_inc(s["pt"], 1)
                return go

            def head_loads(h):
                if not again(h):
                    act.dma_start(kwb[:, :], bass.AP(io["k_norm_w"].tensor, io["k_norm_w"].offset, [[0, P], [1, P]])).then_inc(s["row_load"], 16)
                if again(h):
                    act.wait_ge(s["pv"], 5 * h)
                    act.wait_ge(s["s_out"], 32 * h)
                    act.wait_ge(s["ob"], 5 * h)
                act.dma_start(kc[:, :, :], ck[h, :, :].rearrange("(a p) d -> p a d", p=P)).then_inc(s["cache_load"], 16)
                act.dma_start(vc[:, :, :], cvd[h, :, :].rearrange("(a p) d -> p a d", p=P)).then_inc(s["cache_load"], 16)
                act.dma_start(Ss[:, :], sdelta[h, :, :]).then_inc(s["s_load"], 16)
                rows = relx[h, :]
                act.dma_start(Bp[:, :], bass.AP(rows.tensor, rows.offset, [[1, P], [1, 2 * P]])).then_inc(s["bias_load"], 16)

            def k_store(h):
                act.wait_ge(s["bkw"], h + 1)
                act.dma_start(kv_o["p_k"][h, :, :].rearrange("(t p) d -> p t d", p=P), bk[:, 0:NT, :]).then_inc(s["k_out"], 16)
                act.dma_start(kv_o["s_k"][h, :, :], bk[0:NS, NT, :]).then_inc(s["k_out"], 16)

            def v_store(h):
                act.wait_ge(s["bnat"], h * 3 + 3)
                act.dma_start(kv_o["p_v"][h, :, :].rearrange("(t p) d -> p t d", p=P), bv[:, 0:NT, :]).then_inc(s["v_out"], 16)
                act.dma_start(kv_o["s_v"][h, :, :], bv[0:NS, NT, :]).then_inc(s["v_out"], 16)

            def s_store(h):
                act.wait_ge(s["ss_new"], h * 9 + 9)
                act.dma_start(pdel_o[h, :, :], St[:, :]).then_inc(s["s_out"], 16)
                act.dma_start(sdel_o[h, :, :], Ss[:, :]).then_inc(s["s_out"], 16)

            steps = [(8, a_evac(0)), (16, a_evac(1)), (24, a_evac(2)), (10, a_exp(0)), (18, a_exp(1)), (34, a_exp(2)),
                     (18, a_nat(0)), (24, a_nat(1)), (27, a_lnexp("x_a", "y_a", 0, 2)), (28, a_et),
                     (31, a_trev(knT, 0)), (42, a_nat(2)), (32, gate_evac(3, sga, "ga_z")), (41, gate_exp(sga, "ga_z", "ga_e")), (33, a_trev(qnT, 1)),
                     (34, a_trev(None, 2)), (37, a_m), (55, a_w)]
            for n in range(5):
                steps.append((40 + 3 * n, level_evac("lx_ps", "lx", Xs, 5, n)))
                if n < 4:
                    steps.append((42 + 3 * n, level_evac("lt_ps", "lt", Tm, 4, n)))
            steps += [(59 + 2 * max(n - 1, 0), a_o(n)) for n in range(9)]
            steps += [(76, a_lnexp("x_o", "y_o", 0, 1))]
            steps += [(43, b_evac(0)), (48, b_evac(1)), (56, b_evac(2)), (45, b_nat(0)), (52, b_nat(1)), (59, b_nat(2)),
                      (48, b_ct), (54, a_lnexp("x_b", "y_b", 0, 2)), (58, b_trev(0)), (60, b_trev(1)),
                      (GRID, gate_evac(7, sgb, "gb_z")), (GRID, gate_exp(sgb, "gb_z", "gb_e")), (22, head_loads), (60, k_store), (61, v_store), (76, s_store)]
            steps += [(64 + 4 * i, b_exp(i)) for i in range(5)] + [(69 + 4 * i, b_pt(i)) for i in range(5)]
            steps.sort(key=lambda x: x[0])

            act.dma_start(con[:, :, :], io["con"]).then_inc(s["c_load"], 16)
            act.dma_start(eye[:, :], io["con"][:, IDENT, :]).then_inc(s["c_load"], 16)
            act.dma_start(vrow[0:96, 0, :], io["conv_w"].rearrange("o i (b c) -> (o i b) c", c=P)).then_inc(s["c_load"], 16)
            act.dma_start(vrow[96:112, 0, :], io["norm_w"].rearrange("o (b c) -> (o b) c", c=P)).then_inc(s["c_load"], 16)
            act.dma_start(vrow[112:113, 0, :], io["gdn_norm_w"]).then_inc(s["c_load"], 16)
            act.dma_start(vrow[113:114, 0, :], io["q_norm_w"]).then_inc(s["c_load"], 16)
            act.dma_start(vrow[0:72, 1, :], io["state_conv"].rearrange("o b i (c d) -> (o b i c) d", d=P)).then_inc(s["c_load"], 16)
            act.dma_start(vrow[72:120, 1, :], io["ada_b"].rearrange("o (b c) -> (o b) c", c=P)).then_inc(s["c_load"], 16)
            act.dma_start(crow[0:KT, :], io["c_prompt"].rearrange("b (t d) -> (b t) d", d=P)).then_inc(s["c_load"], 16)
            act.dma_start(crow[KT:2 * KT, :], io["c_sample"].rearrange("b (t d) -> (b t) d", d=P)).then_inc(s["c_load"], 16)

            def x_in(t):
                if t < NT:
                    act.dma_start(xn[t % 2][:, :], x_p[t * P:(t + 1) * P, :]).then_inc(s[f"x_load{t % 2}"], 16)
                else:
                    act.dma_start(xn[t % 2][0:NS, :], x_s).then_inc(s[f"x_load{t % 2}"], 16)
            x_in(0)
            x_in(1)
            act.dma_start(wba[:, :, :], w_in[:, COL_BA:COL_BA + 16].rearrange("(k p) n -> p k n", p=P)).then_inc(s["wba_load"], 16)
            for n, name in enumerate(("gdn_dt_bias", "gdn_a_log")):
                row = io[name]
                act.dma_start(dtb[:, n, :], bass.AP(row.tensor, row.offset, [[0, P], [1, HEADS]])).then_inc(s["row_load"], 16)
            act.wait_ge(s["cT_ps"], 1)
            act.copy(cv[:, :, :].rearrange("p k g -> p g k"), ps[:, G2, 0:2 * KT].rearrange("p (g k) -> p g k", g=2))
            act.activation(ce[:, :], ps[:, G2, 0:2 * KT], ACT.Exp, scale=-1.0).then_inc(s["cT_e"], 1)
            act.wait_ge(s["vec_ps"], 1)
            act.copy(vecT[:, 0, 0:114], ps[:, A1, 0:114])
            act.copy(vecT[:, 1, 0:120], ps[:, A1, P:P + 120]).then_inc(s["vec_sb"], 1)
            for t in range(NT + 1):
                rows = P if t < NT else NS
                act.wait_ge(s[f"x_load{t % 2}"], 16 * (t // 2 + 1))
                act.activation(junk[0:rows, :], xn[t % 2][0:rows, :], ACT.Square, accum_out=xs[0:rows, 0:1]).then_inc(s["x_ss"], 1)
                act.wait_ge(s["x_e"], 2 * t + 1)
                link(act.activation(xs[0:rows, 2:3], xs[0:rows, 1:2], ACT.Ln))
                act.activation(xs[0:rows, 3:4], xs[0:rows, 2:3], ACT.Exp, scale=-0.5).then_inc(s["x_e"], 1)
                for q in range(4):
                    act.wait_ge(s["xt_ps"], 4 * t + q + 1)
                    out = xT[:, 4 * q:4 * q + 4, t * P:t * P + rows]
                    act.copy(out, tiles(G1 + q % 2)[:, :, 0:rows]).then_inc(s["xt"], 1)
                if t + 2 <= NT:
                    x_in(t + 2)
            act.wait_ge(s["wba_load"], 16)
            act.activation(wbs[:, :, 0, :], wba[:, :, :], ACT.Copy).then_inc(s["wba_hi"], 1)
            for k in range(KT):
                act.wait_ge(s["h_full"], k + 1)
                act.activation(Hh[:, k, :], xT[:, k, :], ACT.Copy).then_inc(s["h_hi"], 1)
            for c in range(LEAD):
                split_hi(act, 0, c)
            act.wait_ge(s["ba_ps"], 1)
            act.copy(bar[:, 0:NT, :], ps[:, G1, 0:32 * NT].rearrange("p (t n) -> p t n", n=32))
            act.copy(bar[0:NS, NT, :], ps[P - NS:P, G1, 32 * NT:32 * NT + 32]).then_inc(s["ba_sb"], 1)
            act.wait_ge(s["g_e1"], 1)
            link(act.activation(gt[0][:, :, :], bax[:, 0:HEADS, :], ACT.Exp, scale=-1.0))
            act.activation(gt[2][:, :, :], gt[1][:, :, :], ACT.Exp, scale=-1.0)
            act.activation(dtb[:, 1, :], dtb[:, 1, :], ACT.Exp).then_inc(s["g_e2"], 1)
            act.wait_ge(s["g_e1"], 2)
            act.activation(gt[4][:, :, :], gt[3][:, :, :], ACT.Ln).then_inc(s["g_e3"], 1)
            act.wait_ge(s["cum_ps"], 1)
            act.copy(Gc[:, :, :], ps[:, G2, 0:NG].rearrange("p (h t) -> p h t", h=HEADS))
            act.activation(eG[:, :, :], ps[:, G2, 0:NG].rearrange("p (h t) -> p h t", h=HEADS), ACT.Exp)
            act.copy(gt[0][:, :, :], ps[:, G2, NG:2 * NG].rearrange("p (h t) -> p h t", h=HEADS))
            act.activation(glb[:, :, :, :], ps[:, G2, 2 * NG:4 * NG].rearrange("p (a h t) -> p a h t", a=2, h=HEADS), ACT.Exp).then_inc(s["cum_sb"], 1)
            act.wait_ge(s["cum_d"], 1)
            act.activation(egl[:, :, :], gt[1][:, :, :], ACT.Exp).then_inc(s["gates"], 1)

            def body(h, last=False):
                for place in range(GRID):
                    if place % 2 == 0 and not (last and place // 2 + LEAD >= 32):
                        split_hi(act, h * 32, place // 2 + LEAD)
                    run_head(steps, h, place)
            body(0)
            with act.Fori(1, HEADS - 1) as h:
                link.loop(h, 1, ACT_LINKS)
                body(h)
            link.end(HEADS - 2)
            body(HEADS - 1, True)

            for place in range(32):
                run_tail(steps, place)
            act.wait_ge(s["cs_ps"], 1)
            act.copy(csT[:, 0, :], ps[:, A1, 0:P])
            act.copy(csT[0:16, 1, :], ps[0:16, A1, P:2 * P]).then_inc(s["cs_sb"], 1)
            act.wait_ge(s["cs_sb"], 1)
            pc = io["p_conv"].rearrange("o b i (c d) -> (o b i c) d", d=P)
            sc = io["s_conv"].rearrange("o b i (c d) -> (o b i c) d", d=P)
            act.dma_start(pc, csT[0:72, 0, :]).then_inc(s["cs_out"], 16)
            act.dma_start(sc[0:P - 72, :], csT[72:P, 0, :]).then_inc(s["cs_out"], 16)
            act.dma_start(sc[P - 72:72, :], csT[0:16, 1, :]).then_inc(s["cs_out"], 16)
            act.wait_ge(s["oa"], HEADS)
            act.wait_ge(s["ob"], 5 * HEADS)
            act.wait_ge(s["s_out"], 32 * HEADS)
            act.wait_ge(s["k_out"], 32 * HEADS)
            act.wait_ge(s["v_out"], 32 * HEADS)
            act.wait_ge(s["cs_out"], 16 * 3)
            act.wait_ge(s["ada_cps"], 12)
            for k in range(KT):
                act.activation(Oh[:, k, :], Of[:, k, :], ACT.Copy).then_inc(s["o_hi"], 1)
            for c in range(LEAD):
                split_hi(act, SL_MERGE, c, ADA + ADA_GATE)

            def merge(j):
                for place in range(24):
                    if place % 2 == 0:
                        split_hi(act, j * 12 + SL_MERGE, place // 2 + LEAD, ADA + ADA_GATE)
                    for v in range(2):
                        if place == 8 * v + 8:
                            act.wait_ge(s["used"], j * 12 + SL_MERGE + 4 * (v + 1))
                            if again(j):
                                act.wait_ge(s["mrg"], j)
                            act.activation(halves(sg[v][:, :]), acc(v), ACT.Exp, scale=-1.0).then_inc(s["m_e"], 1)
            merge(0)
            with act.Fori(1, KT) as j:
                merge(j)
            act.wait_ge(s["used"], SL_OUT)
            act.wait_ge(s["mrg"], KT)
            for k in range(KT):
                act.activation(Hh[:, k, :], Of[:, k, :], ACT.Copy).then_inc(s["m_hi"], 1)

            def out_load(j, b):
                act.dma_start(xr[:, b, 0:NT, :], x_p[:, bass.ds(j * P, P)].rearrange("(t p) d -> p t d", p=P)).then_inc(x_tail[b], 16)
                act.dma_start(xr[0:NS, b, NT, :], x_s[:, bass.ds(j * P, P)]).then_inc(x_tail[b], 16)

            def out_unit(i, b, more):
                j = i * 2 + b
                for c in range(4):
                    if more or c + LEAD < 4:
                        split_hi(act, i * 8 + SL_OUT, 4 * b + c + LEAD, ADA + ADA_GATE)
                    if c == 0:
                        if again(i):
                            act.wait_ge(s["f_sb"], i * 2 + (b - 1))
                        out_load(j, b)
                    if c == 1 and (again(i) or b):
                        store(j - 1, 1 - b)

            def store(j, b):
                act.wait_ge(s["f_sb"], j + 1)
                act.dma_start(y_p[:, bass.ds(j * P, P)].rearrange("(t p) d -> p t d", p=P), yo[:, b, 0:NT, :]).then_inc(y_out[b], 16)
                act.dma_start(y_s[:, bass.ds(j * P, P)], yo[0:NS, b, NT, :]).then_inc(y_out[b], 16)
            for i in range(1):
                out_unit(0, 0, True)
                out_unit(0, 1, True)
            with act.Fori(1, KT // 2 - 1) as i:
                out_unit(i, 0, True)
                out_unit(i, 1, True)
            out_unit(KT // 2 - 1, 0, True)
            out_unit(KT // 2 - 1, 1, False)
            store(KT - 1, 1)
            act.wait_ge(s["y_out0"], 16 * KT)
            act.wait_ge(s["y_out1"], 16 * KT)
            act.wait_ge(s["cs_out"], 16 * 3)


        def both(view):
            return view[:, 0:NT, :], view[0:NS, NT, 0:NS]

        def both_ps():
            return tiles(G1), ps[0:NS, G2, 0:NS]

        def const_for(n):
            return con[:, n, :].unsqueeze(1).to_broadcast([P, NT, P]), con[0:NS, n, 0:NS]

        def rows_of(i):
            return P if i < NT else NS

        def keys_of(i):
            return (i + 1) * P if i < NT else PAST + NS

        def scores(i):
            return Pb[i % 2][0:rows_of(i), :, :].rearrange("p a n -> p (a n)")[:, 0:keys_of(i)]

        @block.vector
        def _(dve):
            link = Link(dve, s["dve_link"])
            stt = dve.scalar_tensor_tensor

            def conv(i):
                def go(h):
                    dve.wait_ge(s["cin_ready"], h * 3 + i + 1)
                    if i or again(h):
                        dve.wait_ge(s["act_ready"], h * 3 + i)
                    w = conv_cols[:, h + 8 * i, :]
                    link(dve.tensor_scalar(cacc[:, :], cin[:, 0:N + 3], w[:, 0:1], None, ALU.mult))
                    for tap in (1, 2):
                        link(stt(cacc[:, :], cin[:, tap:tap + N + 3], w[:, tap:tap + 1], cacc[:, :], ALU.mult, ALU.add))
                    stt(cacc[:, :], cin[:, 3:N + 6], w[:, 3:4], cacc[:, :], ALU.mult, ALU.add).then_inc(s["conv_done"], 1)
                return go

            def inverse_in_parts(places, ready, use):
                def part(n):
                    def go(h):
                        if n == 0:
                            ready(h)
                            link(dve.tensor_scalar(eT[:, :], eT[:, :], 1.0, None, ALU.add))
                        cols = slice(n * INV, min((n + 1) * INV, N + 3))
                        link(dve.reciprocal(eT[:, cols], eT[:, cols]))
                    return go
                return [(places[n], part(n)) for n in range(3)] + [(places[3], use)]

            def conv_e(i):
                def ready(h):
                    dve.wait_ge(s["exp_a"], h * 3 + i + 1)
                return ready

            def gate_e(sem):
                def ready(h):
                    dve.wait_ge(s[sem], h + 1)
                return ready

            def silu(i):
                def go(h):
                    if i == 0 and again(h):
                        dve.wait_ge(s["bnat_ps"], h * 3)
                    if i:
                        dve.wait_ge(s["nat_ps"], h * 3 + i)
                    dve.tensor_tensor(aT[:, 0:NP], cacc[:, 0:NP], eT[:, 0:NP], ALU.mult)
                    dve.tensor_tensor(aT[:, NP:N], cacc[:, NP + 3:N + 3], eT[:, NP + 3:N + 3], ALU.mult).then_inc(s["act_ready"], 1)
                return go

            def red_a(i):
                def go(h):
                    dve.wait_ge(s["sq_a"], h * 2 + i + 1)
                    if i == 0 and again(h):
                        dve.wait_ge(s["x_o"], h)
                    dve.tensor_reduce(st[:, SS_Q + i, :], sqb[:, :, :], AX.X, ALU.add).then_inc(s["ss_a"], 1)
                    if i:
                        dve.wait_ge(s["ss_a"], h * 2 + 2)
                        dve.tensor_scalar(st[:, X_Q:X_Q + 2, :], st[:, SS_Q:SS_Q + 2, :], EPS, None, ALU.add).then_inc(s["x_a"], 1)
                return go

            def scales(h):
                dve.wait_ge(s["y_a"], h + 1)
                if again(h):
                    dve.wait_ge(s["pool_a"], h * 5)
                rsqrt_newton(link, dve, st[:, Y_Q:Y_Q + 2, :], st[:, X_Q:X_Q + 2, :], st[:, T_Q:T_Q + 2, :])
                dve.tensor_scalar(st[:, SC_Q, :], st[:, Y_Q, :], float(P) ** -0.5, None, ALU.mult)
                link(dve.tensor_tensor(st[:, SC_KB, :], st[:, Y_K, :], beta[:, h, :], ALU.mult))
                dve.tensor_tensor(st[:, SC_QG, :], st[:, SC_Q, :], eG[:, h, :], ALU.mult)
                dve.tensor_tensor(st[:, SC_KBG, :], st[:, SC_KB, :], eG[:, h, :], ALU.mult)
                dve.tensor_tensor(st[:, SC_KG, :], st[:, Y_K, :], egl[:, h, :], ALU.mult).then_inc(s["scal_a"], 1)
                dve.wait_ge(s["scal_a"], h + 1)
                if again(h):
                    dve.wait_ge(s["pt_ps"], h * 5)
                dve.tensor_tensor(kn[:, :, :], k_nat[:, :, :], wide(st[:, Y_K, :]), ALU.mult).then_inc(s["knb_a"], 1)
                dve.tensor_tensor(kb[:, :, :], k_nat[:, :, :], wide(st[:, SC_KB, :]), ALU.mult).then_inc(s["knb_a"], 1)

            def decay(h):
                dve.wait_ge(s["grow_ps"], h + 1)
                dve.tensor_tensor(ET[:, 0:NT, :], tiles(G1), wide(Gc[:, h, 0:NT]), ALU.subtract)
                link(dve.tensor_tensor(ET[0:NS, NT, 0:NS], ps[0:NS, G2, 0:NS], Gc[0:NS, h, NT:NT + 1].to_broadcast([NS, NS]), ALU.subtract))
                for a, b in zip(both(ET), (s["diff"], None)):
                    ins = dve.tensor_scalar(a, a, 0.0, None, ALU.min)
                ins.then_inc(s["diff"], 1)

            def kb_t(h):
                dve.wait_ge(s["tr_a"], h * 4 + 2)
                dve.tensor_copy(kbT[:, 0:NP], bank(G1))
                dve.tensor_copy(kbT[:, NP:N], ps[:, G2, 0:NS]).then_inc(s["tra_dve"], 1)

            def masked(ps_sem, em, factor, dst, sb_sem):
                def go(h):
                    dve.wait_ge(s[ps_sem], h + 1)
                    dve.wait_ge(s["em"], h * 2 + em)
                    for o, a, b in zip(both(dst), both_ps(), both(factor)):
                        ins = dve.tensor_tensor(o, a, b, ALU.mult)
                    ins.then_inc(s[sb_sem], 1)
                return go

            def first_level(h):
                dve.wait_ge(s["m"], h + 1)
                for src, dst, c in ((MT, Sm, PAIR_T), (Mn, Tm, PAIR)):
                    for o, a, b in zip(both(dst), both(src), const_for(c)):
                        ins = dve.tensor_tensor(o, a, b, ALU.mult)
                link(ins)
                for dst in (Sm, Tm):
                    for o, b in zip(both(dst), const_for(IDENT)):
                        ins = dve.tensor_tensor(o, o, b, ALU.add)
                ins.then_inc(s["st0"], 1)

            def level_sub(n):
                def go(h):
                    dve.wait_ge(s["ly_ps"], h * 5 + n + 1)
                    for o, b in zip(both(Sm), both_ps()):
                        ins = dve.tensor_tensor(o, o, b, ALU.subtract)
                    ins.then_inc(s["ly"], 1)
                return go

            def u_evac(h):
                dve.wait_ge(s["u_ps"], h + 1)
                dve.tensor_copy(U_[:, 0:NT, :], tiles(G1))
                dve.tensor_copy(U_[0:NS, NT, :], ps[0:NS, G2, 0:P]).then_inc(s["u_sb"], 1)

            def chunk(n):
                return (0, NS, NT) if n == 0 else (CH * ((n - 1) % 2), CH, (n - 1) // 2)

            def v_new(n):
                def go(h):
                    r0, rows, t = chunk(n)
                    dve.wait_ge(s["sa_ps"], h * 9 + max(n, 1) + 1)
                    if n == 0:
                        dve.wait_ge(s["u_sb"], h + 1)
                        dve.tensor_tensor(Vs[:, :], U_[0:NS, NT, :], ps[0:NS, G1, P:2 * P], ALU.subtract).then_inc(s["vn"], 1)
                        return
                    dve.tensor_tensor(Vn[r0:r0 + rows, :], U_[r0:r0 + rows, t, :], ps[r0:r0 + rows, G1, 0:P], ALU.subtract).then_inc(s["vn"], 1)
                return go

            def state(n):
                def go(h):
                    r0, rows, t = chunk(n)
                    dve.wait_ge(s["sb_ps"], h * 9 + max(n, 1) + 1)
                    S, new = (St, ps[:, G2, 0:P]) if n else (Ss, ps[:, G2, P:2 * P])
                    stt(S[:, :], S[:, :], glb[:, r0 // CH, h, t:t + 1], new, ALU.mult, ALU.add).then_inc(s["ss_new"], 1)
                return go

            def red_o(h):
                dve.wait_ge(s["sq_o"], h + 1)
                link(dve.tensor_reduce(st[:, SS_Q, :], sqb[:, :, :], AX.X, ALU.add))
                dve.tensor_scalar(st[:, X_Q, :], st[:, SS_Q, :], 1.0 / P, EPS, ALU.mult, ALU.add).then_inc(s["x_o"], 1)

            def norm_o(h):
                dve.wait_ge(s["y_o"], h + 1)
                rsqrt_newton(link, dve, st[:, Y_Q, :], st[:, X_Q, :], st[:, T_Q, :])
                dve.tensor_tensor(o_nat[:, :, :], o_nat[:, :, :], wide(st[:, Y_Q, :]), ALU.mult).then_inc(s["on_o"], 1)

            def out_a(h):
                dve.wait_ge(s["o_ps"], h + 1)
                dve.wait_ge(s["sga"], h + 1)
                stt(Of[:, h, 0:NP], bank(G1), gnw_col, sga[:, 0:NP], ALU.mult, ALU.mult)
                stt(Of[:, h, NP:N], ps[:, G2, 0:NS], gnw_col, sga[:, NP:N], ALU.mult, ALU.mult).then_inc(s["oa"], 1)

            def gate(e_sem, z, sem):
                def go(h):
                    dve.tensor_tensor(z[:, :], z[:, :], eT[:, 0:N], ALU.mult).then_inc(s[sem], 1)
                return go

            def mask_bias(h):
                dve.wait_ge(s["bias_load"], h * 16 + 16)
                dve.memset(Bp[0:CH, 0:CH], MASKED).then_inc(s["bias"], 1)

            def red_b(i):
                def go(h):
                    dve.wait_ge(s["bsq"], h * 2 + i + 1)
                    if i == 0:
                        dve.tensor_reduce(st[:, SS_Q, :], sqb[:, :, :], AX.X, ALU.add).then_inc(s["bss"], 1)
                    else:
                        link(dve.tensor_reduce(st[:, SS_K, :], sqb[:, :, :], AX.X, ALU.add))
                        dve.tensor_scalar(st[:, X_Q:X_Q + 2, :], st[:, SS_Q:SS_Q + 2, :], 1.0 / P, EPS, ALU.mult, ALU.add).then_inc(s["x_b"], 1)
                return go

            def scale_b(h):
                dve.wait_ge(s["y_b"], h + 1)
                rsqrt_newton(link, dve, st[:, Y_Q:Y_Q + 2, :], st[:, X_Q:X_Q + 2, :], st[:, T_Q:T_Q + 2, :])
                link(dve.tensor_scalar(st[:, Y_Q, :], st[:, Y_Q, :], float(P) ** -0.5, None, ALU.mult))
                dve.tensor_tensor(bk[:, :, :], bk[:, :, :], wide(st[:, Y_K, :]), ALU.mult).then_inc(s["bk_y"], 1)
                dve.tensor_tensor(bq[:, :, :], bq[:, :, :], wide(st[:, Y_Q, :]), ALU.mult).then_inc(s["bqn"], 1)

            def soft(i):
                def go(h):
                    rows, n = rows_of(i), keys_of(i)
                    dve.wait_ge(s["qk"], h * 5 + i + 1)
                    if i == 0:
                        dve.wait_ge(s["bias"], h + 1)
                    if i < 2:
                        dve.wait_ge(s["ly_ps"], h * 5 + 5)
                    else:
                        dve.wait_ge(s["pt_ps"], h * 5 + i - 1)
                    p = scores(i)
                    width = {0: P, NT: P + NS}.get(i, 2 * P)
                    at = P if i == 0 else 0
                    near = Bp[0:rows, 2 * P - at - width:2 * P - at]
                    near = bass.AP(near.tensor, near.offset + width - 1, [list(near.ap[0]), [-1, width]])
                    if n > width:
                        dve.tensor_scalar(p[:, 0:n - width], ps[0:rows, A1, 0:n - width], Bp[0:rows, 2 * P - 1:2 * P], None, ALU.add)
                    dve.tensor_tensor(p[:, n - width:n], ps[0:rows, A1, n - width:n], near, ALU.add).then_inc(s["sadd"], 1)
                    dve.wait_ge(s["sadd"], h * 5 + i + 1)
                    dve.tensor_reduce(sm[0:rows, i % 2, 0:1], p, AX.X, ALU.max, negate=True).then_inc(s["smax"], 1)
                return go

            def prob(i):
                def go(h):
                    rows = rows_of(i)
                    dve.wait_ge(s["pexp"], h * 5 + i + 1)
                    link(dve.reciprocal(sm[0:rows, i % 2, 2:3], sm[0:rows, i % 2, 1:2]))
                    dve.tensor_scalar(scores(i), scores(i), sm[0:rows, i % 2, 2:3], None, ALU.mult).then_inc(s["pn"], 1)
                return go

            def out_b(i):
                def go(h):
                    rows = rows_of(i)
                    dve.wait_ge(s["pv"], h * 5 + i + 1)
                    if i == 0:
                        dve.wait_ge(s["sgb"], h + 1)
                    cols = slice(i * P, i * P + rows)
                    dve.tensor_tensor(Of[:, h + HEADS, cols], ps[:, A2, 0:rows], sgb[:, cols], ALU.mult).then_inc(s["ob"], 1)
                return go

            steps = [(9, conv(0)), (17, conv(1)), (33, conv(2)), (22, red_a(0)), (26, red_a(1)), (27, decay), (28, scales), (32, kb_t),
                     (35, masked("mt_ps", 1, ES, MT, "mt")), (36, masked("at_ps", 2, EU, AT, "at")), (38, first_level),
                     (56, u_evac), (75, red_o), (77, norm_o), (80, out_a),
                     (47, red_b(0)), (53, red_b(1)), (55, scale_b), (50, mask_bias)]
            steps += inverse_in_parts((11, 12, 13, 14), conv_e(0), silu(0))
            steps += inverse_in_parts((19, 20, 20, 21), conv_e(1), silu(1))
            steps += inverse_in_parts((35, 36, 37, 39), conv_e(2), silu(2))
            steps += inverse_in_parts((43, 44, 46, 47), gate_e("ga_e"), gate("ga_e", sga, "sga"))
            steps += inverse_in_parts((GRID + 1, GRID + 2, GRID + 3, GRID + 4), gate_e("gb_e"), gate("gb_e", sgb, "sgb"))
            steps += [(41 + 3 * n, level_sub(n)) for n in range(5)]
            steps += [(58 + 2 * max(n - 1, 0), v_new(n)) for n in range(9)] + [(59 + 2 * max(n - 1, 0), state(n)) for n in range(9)]
            steps += [(63 + 4 * i, soft(i)) for i in range(5)] + [(66 + 4 * i, prob(i)) for i in range(5)]
            steps += [(71 + 4 * i, out_b(i)) for i in range(5)]
            steps.sort(key=lambda x: x[0])

            dve.memset(bar[:, :, :], 0.0)
            dve.wait_ge(s["cT_e"], 1)
            link(dve.tensor_scalar(ce[:, :], ce[:, :], 1.0, None, ALU.add))
            link(dve.reciprocal(ce[:, :], ce[:, :]))
            dve.tensor_tensor(cvs[:, :, :], cv[:, :, :], ce[:, :].rearrange("p (g k) -> p k g", g=2), ALU.mult).then_inc(s["cT"], 1)

            def x_norm(t):
                rows = rows_of(t)
                dve.wait_ge(s["x_ss"], t + 1)
                dve.tensor_scalar(xs[0:rows, 1:2], xs[0:rows, 0:1], 1.0 / D, EPS, ALU.mult, ALU.add).then_inc(s["x_e"], 1)
                dve.wait_ge(s["x_e"], 2 * t + 2)
                rsqrt_newton(link, dve, xs[0:rows, 3:4], xs[0:rows, 1:2], xs[0:rows, 4:5])
                dve.tensor_scalar(xn[t % 2][0:rows, :], xn[t % 2][0:rows, :], xs[0:rows, 3:4], None, ALU.mult).then_inc(s["x_n"], 1)

            def mod_row(c):
                dve.wait_ge(s["ada_used"], KT * (c + 1))
                dve.tensor_copy(mrows[c // 8][:, :], ps[0:2, c % 2, :]).then_inc(s["ada_row"], 1)

            def mod_col(c, blk):
                dve.wait_ge(s["ada_cps"], c + 1)
                dve.tensor_tensor(modT[:, blk:blk + 4, :], ps[:, 2, 0:8].rearrange("p (b g) -> p b g", g=2),
                                  adab_cols[:, blk:blk + 4].unsqueeze(2).to_broadcast([P, 4, 2]), ALU.add).then_inc(s["ada_col"], 1)

            def h_blocks(q):
                ks = slice(4 * q, 4 * q + 4)
                dve.wait_ge(s["xt"], 4 * (NT + 1))
                link(dve.tensor_scalar(hA[:, ks, :], modT[:, KT + 4 * q:KT + 4 * q + 4, :], 1.0, None, ALU.add))
                link(dve.tensor_tensor(hA[:, ks, :], hA[:, ks, :], norm_col[:, ks].unsqueeze(2).to_broadcast([P, 4, 2]), ALU.mult))
                for k in range(4 * q, 4 * q + 4):
                    dve.tensor_scalar(xT[:, k, 0:NP], xT[:, k, 0:NP], hA[:, k, 0:1], modT[:, k, 0:1], ALU.mult, ALU.add)
                    dve.tensor_scalar(xT[:, k, NP:N], xT[:, k, NP:N], hA[:, k, 1:2], modT[:, k, 1:2], ALU.mult, ALU.add).then_inc(s["h_full"], 1)

            x_norm(0)
            for c in range(8):
                mod_row(c)
                if c + 1 <= NT:
                    x_norm(c + 1)
                mod_col(c, 4 * (c // 2) + (KT if c % 2 == 0 else 0))
                dve.wait_ge(s["ada_col"], c + 1)
                if c == 5:
                    h_blocks(0)
                if c == 6:
                    h_blocks(1)
                if c == 7:
                    h_blocks(2)
                    h_blocks(3)
            dve.wait_ge(s["wba_hi"], 1)
            dve.tensor_tensor(wbs[:, :, 1, :], wba[:, :, :], wbs[:, :, 0, :].bitcast(F32), ALU.subtract).then_inc(s["wba_lo"], 1)
            for c in range(LEAD):
                split_lo(dve, 0, c)
            dve.wait_ge(s["ba_sb"], 1)
            link(dve.tensor_tensor(bax[:, :, :], bar[:, :, 0:16].rearrange("p t n -> p n t"), bar[:, :, 16:32].rearrange("p t n -> p n t"), ALU.add))
            dve.wait_ge(s["row_load"], 32)
            a_in = bax[:, HEADS:2 * HEADS, :]
            link(dve.tensor_tensor(a_in, a_in, dtb[:, 0, :].unsqueeze(2).to_broadcast(gsz), ALU.add))
            link(dve.tensor_scalar(gt[1][:, :, :], a_in, -1.0, None, ALU.mult))
            dve.tensor_tensor(gt[1][:, :, :], gt[1][:, :, :], a_in, ALU.max).then_inc(s["g_e1"], 1)
            dve.wait_ge(s["g_e2"], 1)
            link(dve.tensor_scalar(gt[0][:, :, :], gt[0][:, :, :], 1.0, None, ALU.add))
            dve.reciprocal(beta[:, :, :], gt[0][:, :, :])
            dve.tensor_scalar(gt[3][:, :, :], gt[2][:, :, :], 1.0, None, ALU.add).then_inc(s["g_e1"], 1)
            dve.wait_ge(s["g_e1"], 2)
            stt(gt[5][:, :, :], gt[3][:, :, :], -1.0, gt[2][:, :, :], ALU.add, ALU.subtract)
            link(dve.reciprocal(gt[0][:, :, :], gt[3][:, :, :]))
            link(dve.tensor_tensor(gt[5][:, :, :], gt[5][:, :, :], gt[0][:, :, :], ALU.mult))
            dve.wait_ge(s["g_e3"], 1)
            link(dve.tensor_tensor(gt[4][:, :, :], gt[4][:, :, :], gt[5][:, :, :], ALU.subtract))
            link(stt(gt[4][:, :, :], a_in, 0.0, gt[4][:, :, :], ALU.max, ALU.add))
            link(stt(gg[:, :, :], gt[4][:, :, :], -1.0, dtb[:, 1, :].unsqueeze(2).to_broadcast(gsz), ALU.mult, ALU.mult))
            dve.memset(gg[NS:2 * NS, :, NT], 0.0)
            dve.memset(gg[2 * NS:P, :, NT], 0.0).then_inc(s["g_g"], 1)
            dve.wait_ge(s["cum_sb"], 1)
            dve.tensor_tensor(gt[1][:, :, :], gt[0][:, :, :], Gc[:, :, :], ALU.subtract).then_inc(s["cum_d"], 1)

            def body(h, last=False):
                for place in range(GRID):
                    if place % 2 == 0 and not (last and place // 2 + LEAD >= 32):
                        split_lo(dve, h * 32, place // 2 + LEAD)
                    run_head(steps, h, place)
            body(0)
            with dve.Fori(1, HEADS - 1) as h:
                link.loop(h, 1, DVE_LINKS)
                body(h)
            link.end(HEADS - 2)
            body(HEADS - 1, True)

            for place in range(32):
                run_tail(steps, place)
                if place % 8 == 7:
                    mod_row(8 + place // 8)
                if place % 8 == 1 and place > 8:
                    mod_col(8 + place // 8 - 1, 2 * KT + 4 * (place // 8 - 1))
            mod_col(11, 2 * KT + 12)
            for k in range(KT):
                dve.wait_ge(s["o_hi"], k + 1)
                dve.tensor_tensor(Ol[:, k, :], Of[:, k, :], Oh[:, k, :].bitcast(F32), ALU.subtract).then_inc(s["o_lo"], 1)
            for c in range(LEAD):
                split_lo(dve, SL_MERGE, c)

            def merge(j):
                for place in range(24):
                    if place % 2 == 0:
                        split_lo(dve, j * 12 + SL_MERGE, place // 2 + LEAD)
                    for v in range(2):
                        if place == 8 * v + 9:
                            dve.wait_ge(s["m_e"], j * 2 + v + 1)
                            link(dve.tensor_scalar(sg[v][:, :], sg[v][:, :], 1.0, None, ALU.add))
                            dve.reciprocal(sg[v][:, :], sg[v][:, :]).then_inc(s["m_sig"], 1)
                    if place == 20:
                        dve.wait_ge(s["used"], j * 12 + SL_MERGE + 10)
                        dve.wait_ge(s["m_sig"], j * 2 + 2)
                        dve.tensor_tensor(halves(tmp[:, :]), acc(0), halves(sg[0][:, :]), ALU.mult).then_inc(s["mrg_a"], 1)
                dve.wait_ge(s["used"], j * 12 + SL_MERGE + 12)
                link(dve.tensor_tensor(halves(sg[1][:, :]), acc(1), halves(sg[1][:, :]), ALU.mult))
                dve.tensor_tensor(Of[:, j, :], tmp[:, :], sg[1][:, :], ALU.add).then_inc(s["mrg"], 1)
            merge(0)
            with dve.Fori(1, KT) as j:
                link.loop(j, 1, 3)
                merge(j)
            link.end(KT - 1)
            for k in range(KT):
                dve.wait_ge(s["m_hi"], k + 1)
                dve.tensor_tensor(Hl[:, k, :], Of[:, k, :], Hh[:, k, :].bitcast(F32), ALU.subtract).then_inc(s["m_lo"], 1)

            def out_unit(i, b, more):
                j = i * 2 + b
                for c in range(4):
                    if more or c + LEAD < 4:
                        split_lo(dve, i * 8 + SL_OUT, 4 * b + c + LEAD)
                    if c == 1 and b:
                        residual(i, 0)
                    if c == 1 and not b and again(i):
                        residual(i - 1, 1)
                dve.wait_ge(s["used"], j * 4 + SL_OUT + 4)
                if again(i):
                    dve.wait_ge(s["f_ps"], j - 1)
                gcol = modT[:, j + 2 * KT, :]
                dve.tensor_scalar(fo[:, b, 0:HALF], ps[:, 2 * b, 0:HALF], gcol[:, 0:1], None, ALU.mult)
                dve.tensor_scalar(fo[:, b, HALF:NP], ps[:, 2 * b + 1, 0:NP - HALF], gcol[:, 0:1], None, ALU.mult)
                dve.tensor_scalar(fo[:, b, NP:N], ps[:, 2 * b + 1, NP - HALF:HALF], gcol[:, 1:2], None, ALU.mult).then_inc(s["f_g"], 1)

            def residual(i, b, first=False):
                dve.wait_ge(s["f_ps"], i * 2 + b + 1)
                dve.wait_ge(x_tail[b], i * 32 + 32)
                if again(i) and not first:
                    dve.wait_ge(y_out[b], i * 32)
                dve.tensor_tensor(yo[:, b, 0:NT, :], tiles(G1), xr[:, b, 0:NT, :], ALU.add)
                dve.tensor_tensor(yo[0:NS, b, NT, :], ps[0:NS, G2, 0:P], xr[0:NS, b, NT, :], ALU.add).then_inc(s["f_sb"], 1)
            out_unit(0, 0, True)
            out_unit(0, 1, True)
            with dve.Fori(1, KT // 2 - 1) as i:
                out_unit(i, 0, True)
                out_unit(i, 1, True)
            out_unit(KT // 2 - 1, 0, True)
            out_unit(KT // 2 - 1, 1, False)
            residual(KT // 2 - 1, 1)

        @block.gpsimd
        def _(pool):
            mul = ALU.mult

            def tails(i):
                def go(h):
                    pool.wait_ge(s["cin_ready"], h * 3 + i + 1)
                    pool.tensor_copy(cs[:, 0:3, h + 8 * i], cin[:, NP:NP + 3])
                    pool.tensor_copy(cs[:, 3:6, h + 8 * i], cin[:, N + 3:N + 6]).then_inc(s["tails"], 1)
                return go

            def square_a(i):
                def go(h):
                    src = (q_nat, k_nat)[i]
                    pool.wait_ge(s["nat_a"], h * 3 + i + 1)
                    if i:
                        pool.wait_ge(s["ss_a"], h * 2 + 1)
                    elif again(h):
                        pool.wait_ge(s["x_o"], h)
                    pool.tensor_tensor(sqb[:, :, :], src[:, :, :], src[:, :, :], mul).then_inc(s["sq_a"], 1)
                return go

            def g_wide(h):
                if again(h):
                    pool.wait_ge(s["pt_ps"], h * 5)
                pool.tensor_copy(gbc[:, :, :], wide(gg[:, h, :])).then_inc(s["gbc"], 1)

            def scaled(h):
                pool.wait_ge(s["scal_a"], h + 1)
                if again(h):
                    pool.wait_ge(s["sb_ps"], h * 9)
                for dst, src, c in ((qn, q_nat, SC_Q), (qg, q_nat, SC_QG), (kbg, k_nat, SC_KBG), (kg, k_nat, SC_KG)):
                    pool.tensor_tensor(dst[:, :, :], src[:, :, :], wide(st[:, c, :]), mul).then_inc(s["pool_a"], 1)

            def scaled_v(h):
                pool.wait_ge(s["nat_a"], h * 3 + 3)
                pool.tensor_tensor(vb[:, :, :], v_nat[:, :, :], wide(beta[:, h, :]), mul).then_inc(s["pool_a"], 1)

            def zero_state(h):
                if again(h):
                    pool.wait_ge(s["s_out"], h * 32)
                pool.tensor_tensor(St[:, :], eye[:, :], eye[:, :], ALU.subtract).then_inc(s["s_zero"], 1)

            def mask_decay(h):
                pool.wait_ge(s["et"], h + 1)
                for dst, c in ((ES, STRICT), (EU, UPPER)):
                    for o, a, b in zip(both(dst), both(ET), const_for(c)):
                        ins = pool.tensor_tensor(o, a, b, mul)
                    ins.then_inc(s["em"], 1)

            def level_mask(n):
                def go(h):
                    if n == 0:
                        pool.wait_ge(s["m"], h + 1)
                    if n >= 2:
                        pool.wait_ge(s["lx_ps"], h * 5 + n - 1)
                    for o, a, b in zip(both((B0, B1)[n % 2]), both(Mn), const_for(LEVEL2 + n)):
                        ins = pool.tensor_tensor(o, a, b, mul)
                    ins.then_inc(s["bm"], 1)
                return go

            def square_o(h):
                pool.wait_ge(s["so"], h * 9 + 9)
                pool.wait_ge(s["x_b"], h + 1)
                pool.tensor_tensor(sqb[:, :, :], o_nat[:, :, :], o_nat[:, :, :], mul).then_inc(s["sq_o"], 1)

            def square_b(i):
                def go(h):
                    src = (bq, bk)[i]
                    pool.wait_ge(s["bnat"], h * 3 + i + 1)
                    if i:
                        pool.wait_ge(s["bss"], h + 1)
                    pool.tensor_tensor(sqb[:, :, :], src[:, :, :], src[:, :, :], mul).then_inc(s["bsq"], 1)
                return go

            def k_weight(h):
                pool.wait_ge(s["bk_y"], h + 1)
                if not again(h):
                    pool.wait_ge(s["row_load"], 48)
                pool.tensor_tensor(bk[:, :, :], bk[:, :, :], kwb[:, :].unsqueeze(1).to_broadcast([P, NT + 1, P]), mul).then_inc(s["bkw"], 1)

            steps = [(9, tails(0)), (17, tails(1)), (25, tails(2)), (19, square_a(0)), (25, square_a(1)), (21, g_wide),
                     (28, scaled), (43, scaled_v), (31, zero_state), (31, mask_decay), (74, square_o),
                     (46, square_b(0)), (52, square_b(1)), (56, k_weight)]
            steps += [(38 + 3 * n, level_mask(n)) for n in range(5)]
            steps.sort(key=lambda x: x[0])

            for k in range(KT):
                pool.wait_ge(s["h_hi"], k + 1)
                pool.tensor_tensor(Hl[:, k, :], xT[:, k, :], Hh[:, k, :].bitcast(F32), ALU.subtract).then_inc(s["h_lo"], 1)
            pool.wait_ge(s["gates"], 1)
            for b in (q_nat, k_nat, v_nat, sqb, Mn, B0, B1, MT, AT, Sm, Tm, Xs, vb, kbg, kg, bv):
                pool.memset(b[:, NT, :], 0.0)
            pool.memset(cin[:, 0:3], 0.0).then_inc(s["zeroed"], 1)
            pool.wait_ge(s["zeroed"], 1)

            def body(h):
                for place in range(GRID):
                    run_head(steps, h, place)
            body(0)
            with pool.Fori(1, HEADS) as h:
                body(h)
            for place in range(32):
                run_tail(steps, place)

        @block.tensor
        def _(pe):
            mm = pe.matmul

            def turn(out, in_, rows=P):
                return pe.transpose(out, in_, eye[0:rows, 0:rows])

            def to_nat(src, b):
                for t in range(NT):
                    turn(ps[:, b, t * P:(t + 1) * P], src[:, t * P:(t + 1) * P])
                return turn(ps[0:NS, b + 1, 0:P], src[:, NP:N])

            def to_T(src, b):
                for t in range(NT):
                    turn(ps[:, b, t * P:(t + 1) * P], src[:, t, :])
                return turn(ps[:, b + 1, 0:NS], src[0:NS, NT, :], NS)

            def nat_a(i):
                def go(h):
                    pe.wait_ge(s["act_ready"], h * 3 + i + 1)
                    if i == 0 and again(h):
                        pe.wait_ge(s["oa"], h)
                    if i == 1:
                        pe.wait_ge(s["nat_a"], h * 3 + 1)
                    if i == 2 and again(h):
                        pe.wait_ge(s["ob"], h * 5)
                    to_nat(aT, G1 if i < 2 else A1).then_inc(s["nat_ps"], 1)
                return go

            def grow(h):
                pe.wait_ge(s["gbc"], h + 1)
                pe.wait_ge(s["nat_a"], h * 3 + 2)
                for t in range(NT):
                    mm(ps[:, G1, t * P:(t + 1) * P], gbc[:, t, :], con[:, UPPER, :], start=True, stop=True)
                mm(ps[0:NS, G2, 0:NS], gbc[0:NS, NT, 0:NS], con[0:NS, UPPER, 0:NS], start=True, stop=True).then_inc(s["grow_ps"], 1)

            def tr_a(n):
                def go(h):
                    if n == 0:
                        pe.wait_ge(s["knb_a"], h * 2 + 1)
                        pe.wait_ge(s["diff"], h + 1)
                    if n == 1:
                        pe.wait_ge(s["knb_a"], h * 2 + 2)
                        pe.wait_ge(s["tra_act"], h * 3 + 1)
                    if n == 2:
                        pe.wait_ge(s["pool_a"], h * 5 + 1)
                        pe.wait_ge(s["tra_dve"], h + 1)
                    if n == 3:
                        pe.wait_ge(s["pool_a"], h * 5 + 2)
                        pe.wait_ge(s["tra_act"], h * 3 + 2)
                    to_T((kn, kb, qn, qg)[n], G1).then_inc(s["tr_a"], 1)
                return go

            def outer(right, wait_sem, per, count, sem):
                def go(h):
                    pe.wait_ge(s[wait_sem], h * per + count)
                    for t in range(NT):
                        c = slice(t * P, (t + 1) * P)
                        mm(ps[:, G1, c], knT[:, c], right[:, c], start=True, stop=True)
                    mm(ps[0:NS, G2, 0:NS], knT[:, NP:N], right[:, NP:N], start=True, stop=True).then_inc(s[sem], 1)
                return go

            def turn_square(src):
                for t in range(NT):
                    turn(ps[:, G1, t * P:(t + 1) * P], src[:, t, :])
                return turn(ps[0:NS, G2, 0:NS], src[0:NS, NT, 0:NS], NS)

            def m_turn(h):
                pe.wait_ge(s["at"], h + 1)
                turn_square(MT).then_inc(s["m_ps"], 1)

            def square_product(left, right):
                for t in range(NT):
                    mm(ps[:, G1, t * P:(t + 1) * P], left[:, t, :], right[:, t, :], start=True, stop=True)
                return mm(ps[0:NS, G2, 0:NS], left[0:NS, NT, 0:NS], right[0:NS, NT, 0:NS], start=True, stop=True)

            def level_x(n):
                def go(h):
                    if n == 0:
                        pe.wait_ge(s["st0"], h + 1)
                    else:
                        pe.wait_ge(s["lt"], h * 4 + n)
                    pe.wait_ge(s["bm"], h * 5 + n + 1)
                    square_product((B0, B1)[n % 2], Sm).then_inc(s["lx_ps"], 1)
                return go

            def level_y(n):
                def go(h):
                    pe.wait_ge(s["lx"], h * 5 + n + 1)
                    square_product(Tm, Xs).then_inc(s["ly_ps"], 1)
                return go

            def level_t(n):
                def go(h):
                    pe.wait_ge(s["ly"], h * 5 + n + 1)
                    turn_square(Sm).then_inc(s["lt_ps"], 1)
                return go

            def w_rows(h):
                pe.wait_ge(s["ly"], h * 5 + 5)
                pe.wait_ge(s["pool_a"], h * 5 + 5)
                for t in range(NT):
                    mm(ps[:, G1, t * P:(t + 1) * P], kbg[:, t, :], Sm[:, t, :], start=True, stop=True)
                mm(ps[:, G2, 0:NS], kbg[0:NS, NT, :], Sm[0:NS, NT, 0:NS], start=True, stop=True).then_inc(s["w_ps"], 1)

            def u_rows(h):
                pe.wait_ge(s["w_sb"], h + 1)
                for t in range(NT):
                    mm(ps[:, G1, t * P:(t + 1) * P], Sm[:, t, :], vb[:, t, :], start=True, stop=True)
                mm(ps[0:NS, G2, 0:P], Sm[0:NS, NT, 0:NS], vb[0:NS, NT, :], start=True, stop=True).then_inc(s["u_ps"], 1)

            def chunk_state(n):
                def go(h):
                    if n == 1:
                        pe.wait_ge(s["u_sb"], h + 1)
                        pe.wait_ge(s["s_zero"], h + 1)
                    else:
                        pe.wait_ge(s["so"], h * 9 + n)
                        pe.wait_ge(s["ss_new"], h * 9 + n)
                    mm(ps[:, G1, 0:P], qgw[:, (n - 1) * P:n * P], St[:, :], start=True, stop=True).then_inc(s["sa_ps"], 1)
                    if n == 1:
                        pe.wait_ge(s["s_load"], h * 16 + 16)
                        mm(ps[0:2 * NS, G1, P:2 * P], qgw[:, NCH * P:NCH * P + 2 * NS], Ss[:, :], start=True, stop=True).then_inc(s["sa_ps"], 1)
                return go

            def chunk_new(n):
                def go(h):
                    pe.wait_ge(s["vn"], h * 9 + n + 1)
                    if n == 1:
                        mm(ps[:, G2, P:2 * P], kg[0:NS, NT, :], Vs[:, :], start=True, stop=True)
                        mm(ps[NS:2 * NS, G1, P:2 * P], AT[0:NS, NT, 0:NS], Vs[:, :], start=False, stop=True, skip_group_check=True).then_inc(s["sb_ps"], 1)
                    r0 = CH * ((n - 1) % 2)
                    o0, rows, t = CH - r0, CH, (n - 1) // 2
                    k = slice(r0, r0 + rows)
                    mm(ps[:, G2, 0:P], kg[k, t, :], Vn[k, :], start=True, stop=True)
                    mm(ps[o0:o0 + rows, G1, 0:P], AT[k, t, k], Vn[k, :], start=False, stop=True, skip_group_check=True).then_inc(s["sb_ps"], 1)
                return go

            def o_turn(h):
                pe.wait_ge(s["on_o"], h + 1)
                to_T(o_nat, G1).then_inc(s["o_ps"], 1)

            def nat_b(i):
                def go(h):
                    pe.wait_ge(s["bz"], h * 3 + i + 1)
                    if i == 0:
                        pe.wait_ge(s["nat_a"], h * 3 + 3)
                    if i == 1:
                        pe.wait_ge(s["ct"], h + 1)
                    if i == 2:
                        pe.wait_ge(s["btr"], h * 2 + 1)
                    to_nat(aT, A1).then_inc(s["bnat_ps"], 1)
                return go

            def cache_turn(h):
                pe.wait_ge(s["cache_load"], h * 32 + 32)
                pe.wait_ge(s["bnat"], h * 3 + 1)
                for a in range(2):
                    ins = turn(ps[:, A1, a * P:(a + 1) * P], kc[:, a, :])
                ins.then_inc(s["ct_ps"], 1)

            def tr_b(n):
                def go(h):
                    if n == 0:
                        pe.wait_ge(s["bkw"], h + 1)
                        pe.wait_ge(s["bnat"], h * 3 + 2)
                    else:
                        pe.wait_ge(s["bqn"], h + 1)
                        pe.wait_ge(s["bnat"], h * 3 + 3)
                    to_T((bk, bq)[n], A1).then_inc(s["btr_ps"], 1)
                return go

            def score(i):
                def go(h):
                    if i == 0:
                        pe.wait_ge(s["btr"], h * 2 + 2)
                    else:
                        pe.wait_ge(s["sadd"], h * 5 + i)
                    if i < NT:
                        ins = mm(ps[:, A1, 0:(i + 1) * P], qT[:, i * P:(i + 1) * P], kT[:, 0:(i + 1) * P], start=True, stop=True)
                    else:
                        mm(ps[0:NS, A1, 0:PAST], qT[:, NP:N], kcT[:, :], start=True, stop=True)
                        ins = mm(ps[0:NS, A1, PAST:PAST + NS], qT[:, NP:N], kT[:, NP:N], start=True, stop=True)
                    ins.then_inc(s["qk"], 1)
                return go

            def prob_turn(i):
                def go(h):
                    pe.wait_ge(s["pn"], h * 5 + i + 1)
                    if i:
                        pe.wait_ge(s["ob"], h * 5 + i)
                    p = scores(i)
                    if i < NT:
                        for t in range(i + 1):
                            ins = turn(ps[:, A2, t * P:(t + 1) * P], p[:, t * P:(t + 1) * P])
                    else:
                        mm(ps[:, A2, 0:NS], p[:, 0:P], eye[0:NS, 0:NS], start=True, stop=True)
                        turn(ps[:, A2, NS:2 * NS], p[:, P:2 * P], NS)
                        ins = turn(ps[0:NS, A2, 2 * NS:3 * NS], p[:, PAST:PAST + NS], NS)
                    ins.then_inc(s["pt_ps"], 1)
                return go

            def values(i):
                def go(h):
                    pe.wait_ge(s["pt"], h * 5 + i + 1)
                    if i < NT:
                        for t in range(i + 1):
                            ins = mm(ps[:, A2, 0:P], bv[:, t, :], PT[:, t * P:(t + 1) * P], start=t == 0, stop=t == i)
                    else:
                        for t in range(2):
                            mm(ps[:, A2, 0:NS], vc[:, t, :], PT[:, t * NS:(t + 1) * NS], start=t == 0, stop=False)
                        ins = mm(ps[:, A2, 0:NS], bv[0:NS, NT, :], PT[0:NS, 2 * NS:3 * NS], start=False, stop=True)
                    ins.then_inc(s["pv"], 1)
                return go

            steps = [(17, nat_a(0)), (23, nat_a(1)), (26, grow), (31, tr_a(0)), (42, nat_a(2)), (32, tr_a(1)), (33, tr_a(2)),
                     (34, tr_a(3)), (35, outer(kbT, "tra_act", 3, 3, "mt_ps")), (36, outer(qnT, "mt", 1, 1, "at_ps")), (37, m_turn),
                     (55, w_rows), (56, u_rows), (79, o_turn),
                     (45, nat_b(0)), (48, cache_turn), (51, nat_b(1)), (58, tr_b(0)), (59, nat_b(2)), (60, tr_b(1))]
            for n in range(5):
                steps += [(40 + 3 * n, level_x(n)), (41 + 3 * n, level_y(n))]
                if n < 4:
                    steps.append((42 + 3 * n, level_t(n)))
            steps += [(58 + 2 * n, chunk_state(n + 1)) for n in range(8)] + [(59 + 2 * n, chunk_new(n + 1)) for n in range(8)]
            steps += [(62 + 4 * i, score(i)) for i in range(5)] + [(68 + 4 * i, prob_turn(i)) for i in range(5)]
            steps += [(70 + 4 * i, values(i)) for i in range(5)]
            steps.sort(key=lambda x: x[0])

            def products(base, c, half, Xh, Xl, k0, pair, start, stop):
                r = c % RING
                if half == 0:
                    pe.wait_ge(s["lo"], base + (c + 1))
                for n in range(2):
                    w = slice((2 * half + n) * P, (2 * half + n + 1) * P)
                    k = k0 + n
                    passes = [(whi, Xh), (whi, Xl), (wlo, Xh)]
                    for m, (weights, X) in enumerate(passes):
                        for a in range(2):
                            ins = mm(ps[:, 2 * pair + a, 0:HALF], weights[:, r, w], X[:, k, a * HALF:(a + 1) * HALF],
                                     start=start and n == 0 and m == 0, stop=stop and n == 1 and m == 2)
                if half == 1:
                    ins.then_inc(s["used"], 1)

            pe.wait_ge(s["c_load"], 16 * 10)
            turn(ps[:, A1, 0:114], vrow[0:114, 0, :], 114)
            turn(ps[:, A1, P:P + 120], vrow[0:120, 1, :], 120).then_inc(s["vec_ps"], 1)
            turn(ps[:, G2, 0:2 * KT], crow[:, :], 2 * KT).then_inc(s["cT_ps"], 1)

            def ada_slot(m, c, k):
                if m == 0:
                    pe.wait_ge(s["cT"], 1)
                if k == 0 and c >= 2:
                    pe.wait_ge(s["ada_row"], c - 1)
                pe.wait_ge(landed[m % RING], 16 * (m // RING + 1))
                mm(ps[0:2, c % 2, :], cvs[:, k, :], raw[:, m % RING, :], start=k == 0, stop=k == KT - 1).then_inc(s["ada_used"], 1)

            def mod_turn(c):
                pe.wait_ge(s["ada_row"], c + 1)
                if c:
                    pe.wait_ge(s["ada_col"], c)
                for b in range(4):
                    ins = mm(ps[:, 2, 2 * b:2 * b + 2], mrows[c // 8][:, b * P:(b + 1) * P], eye[0:2, 0:2], start=True, stop=True)
                ins.then_inc(s["ada_cps"], 1)

            for c in range(8):
                for k in range(KT):
                    ada_slot(KT * c + k, c, k)
                    if k == 3 and c:
                        mod_turn(c - 1)
                if c <= NT:
                    rows = rows_of(c)
                    pe.wait_ge(s["x_n"], c + 1)
                    for q in range(4):
                        if 4 * c + q >= 2:
                            pe.wait_ge(s["xt"], 4 * c + q - 1)
                        for b in range(4):
                            k = 4 * q + b
                            ins = turn(ps[:, G1 + q % 2, b * P:b * P + rows], xn[c % 2][0:rows, k * P:(k + 1) * P], rows)
                        ins.then_inc(s["xt_ps"], 1)
            mod_turn(7)
            pe.wait_ge(s["wba_lo"], 1)
            pe.wait_ge(s["h_lo"], KT)
            for t in range(NT + 1):
                c0 = t * P if t < NT else N - P
                for k in range(KT):
                    mm(ps[:, G1, 32 * t:32 * t + 32], Hh[:, k, c0:c0 + P], wbs[:, k, :, :].rearrange("p a n -> p (a n)"),
                       start=k == 0, stop=k == KT - 1)
                    ins = mm(ps[:, G1, 32 * t:32 * t + 16], Hl[:, k, c0:c0 + P], wbs[:, k, 0, :], start=False, stop=k == KT - 1,
                             skip_group_check=True)
            ins.then_inc(s["ba_ps"], 1)

            def cumulate():
                pe.wait_ge(s["g_g"], 1)
                g = gg[:, :, :].rearrange("p h t -> p (h t)")
                for n, c in enumerate((UPPER, BLOCK, ROWS_A, ROWS_B)):
                    ins = mm(ps[:, G2, n * NG:(n + 1) * NG], con[:, c, :], g, start=True, stop=True)
                ins.then_inc(s["cum_ps"], 1)

            def pair_free(u, h):
                if u == 0 and again(h):
                    pe.wait_ge(s["bz"], h * 3)
                if u == 0 and not again(h):
                    pe.wait_ge(s["ada_row"], 8)
                if u == 1:
                    if again(h):
                        pe.wait_ge(s["gb_z"], h)
                    else:
                        pe.wait_ge(s["ada_col"], 8)
                if 2 <= u <= 4:
                    pe.wait_ge(s["cin_ready"], h * 3 + u - 1)
                if u == 5:
                    pe.wait_ge(s["ga_z"], h + 1)
                if u >= 6:
                    pe.wait_ge(s["bz"], h * 3 + u - 5)

            def body(h):
                for place in range(GRID):
                    u, part = divmod(place, 8)
                    if part == 0 and u > 0:
                        pair_free(u, h)
                    if place == 0 and not again(h):
                        pair_free(0, h)
                    if place == 0 and again(h):
                        pair_free(0, h)
                    products(h * 32, place // 2, place % 2, Hh, Hl, 2 * part, u % 2, part == 0, part == 7)
                    if place == 2 and not again(h):
                        cumulate()
                    run_head(steps, h, place)
            body(0)
            with pe.Fori(1, HEADS) as h:
                body(h)

            for g in range(ADA_GATE):
                c, k = 8 + g // KT, g % KT
                if g == 0:
                    pe.wait_ge(s["bz"], 3 * HEADS)
                ada_slot(ADA + 32 * HEADS + g, c, k)
                if k == 3 and c > 8:
                    pe.wait_ge(s["gb_z"], HEADS)
                    mod_turn(c - 1)
                if g % 2 == 0:
                    run_tail(steps, g // 2)
            mod_turn(11)
            pe.wait_ge(s["tails"], 3 * HEADS)
            csr = cs[:, :, :].rearrange("p i b -> p (i b)")
            pe.wait_ge(s["sadd"], 5 * HEADS)
            turn(ps[:, A1, 0:P], csr[:, 0:P])
            turn(ps[0:16, A1, P:2 * P], csr[:, P:P + 16]).then_inc(s["cs_ps"], 1)

            def merge(j):
                for u, (c0, count, Xh, Xl, k0) in enumerate(((0, 4, Hh, Hl, 0), (4, 4, Hh, Hl, 0), (8, 2, Oh, Ol, 0), (10, 2, Oh, Ol, 8))):
                    if u < 2:
                        if again(j):
                            pe.wait_ge(s["mrg_a" if u == 0 else "mrg"], j)
                        else:
                            pe.wait_ge(s["ada_row"] if u == 0 else s["ada_col"], 12)
                    else:
                        pe.wait_ge(s["m_e"], j * 2 + u - 1)
                        if not again(j):
                            pe.wait_ge(s["o_lo"], KT)
                    for n in range(2 * count):
                        products(j * 12 + SL_MERGE, c0 + n // 2, n % 2, Xh, Xl, k0 + 2 * n, u % 2, n == 0, n == 2 * count - 1)
            merge(0)
            with pe.Fori(1, KT) as j:
                merge(j)

            def out_turn(j, b):
                pe.wait_ge(s["f_g"], j + 1)
                if again(j):
                    pe.wait_ge(s["f_sb"], j)
                to_nat(fo[:, b, :], G1).then_inc(s["f_ps"], 1)

            def out_unit(i, b):
                j = i * 2 + b
                if again(i):
                    pe.wait_ge(s["f_g"], j - 1)
                else:
                    pe.wait_ge(s["mrg_a" if b == 0 else "mrg"], KT)
                for n in range(8):
                    if not again(i) and b == 0:
                        pe.wait_ge(s["m_lo"], 2 * n + 2)
                    products(i * 8 + SL_OUT, 4 * b + n // 2, n % 2, Hh, Hl, 2 * n, b, n == 0, n == 7)
                    if n == 1 and (again(i) or b):
                        out_turn(j - 1, 1 - b)
            out_unit(0, 0)
            out_unit(0, 1)
            with pe.Fori(1, KT // 2) as i:
                out_unit(i, 0)
                out_unit(i, 1)
            out_turn(KT - 1, 1)


ACT_LINKS = 3
DVE_LINKS = 52

_INS = ["x_prompt", "x_sample", "c_prompt", "c_sample", "state_conv", "state_delta", "cache_k", "cache_v", "norm_w", "ada_w",
        "ada_b", "w_in", "conv_w", "gdn_a_log", "gdn_dt_bias", "gdn_norm_w", "q_norm_w", "k_norm_w", "rel_bias", "w_proj_a",
        "w_proj_b", "w_out"]
_OUTS = {"y_prompt": (1, NP, D), "y_sample": (1, NS, D), "p_conv": (1, 1, 3, 3 * QK), "p_delta": (1, 1, HEADS, P, P),
         "p_k": (1, 1, NP, HEADS, P), "p_v": (1, 1, NP, HEADS, P), "s_conv": (1, 1, 3, 3 * QK),
         "s_delta": (1, 1, HEADS, P, P), "s_k": (1, 1, NS, HEADS, P), "s_v": (1, 1, NS, HEADS, P)}


def kernel(**inputs):
    import concourse.bacc as bacc
    from concourse.bass_utils import run_bass_kernel_spmd

    nc = bacc.Bacc("TRN2", target_bir_lowering=False, num_devices=1)
    arrays = {n: np.ascontiguousarray(inputs[n]) for n in _INS}
    rel = arrays.pop("rel_bias")[0]
    arrays["rel_ext"] = np.ascontiguousarray(np.concatenate([rel[:, 1:], np.repeat(rel[:, -1:], P - 1, axis=1)], axis=1))
    arrays["con"] = constants()
    io = {n: nc.dram_tensor(f"in_{n}", a.shape, mybir.dt.from_np(a.dtype), kind="ExternalInput").ap() for n, a in arrays.items()}
    for n, shape in _OUTS.items():
        io[n] = nc.dram_tensor(f"out_{n}", shape, F32, kind="ExternalOutput").ap()
    hybrid_layer(nc, io)
    r = run_bass_kernel_spmd(nc, [{f"in_{n}": a for n, a in arrays.items()}], core_ids=[0])
    return tuple(r.results[0][f"out_{n}"] for n in _OUTS)
```

```python
from contextlib import ExitStack

import numpy as np

import concourse.bass as bass
from concourse import mybir

F32 = mybir.dt.float32
F32R = mybir.dt.float32r
ACT = mybir.ActivationFunctionType
ALU = mybir.AluOpType
AX = mybir.AxisListType

P = 128
D = 2048
NP = 512
NS = 32
N = NP + NS
HALF = N // 2
KT = D // P
HEADS = 8
NT = NP // P
CH = 64
NCH = NP // CH
EPS = 1e-6
QK = HEADS * P
COL_BA = 4 * QK
COL_B = COL_BA + 2 * HEADS
COL_M = COL_B + 4 * QK
IN_DIM = COL_M + 2 * D
RING = 4
RING_START = 8
RING_PARTS = 6
LEAD_START = 4
SLOT = 512
LEAD = 2
GRID = 64
PAST = 256
MASKED = -1e30
INV = 110
EXP_LN_SET = 6

IDENT, UPPER, BLOCK, STRICT, PAIR_T, PAIR, LEVEL2 = 0, 1, 2, 3, 4, 5, 6
LEVELS = (2, 3, 4, 5, 6)
ROWS_A, ROWS_B = LEVEL2 + len(LEVELS), LEVEL2 + len(LEVELS) + 1
NCONST = ROWS_B + 1


def constants():
    i = np.arange(P)
    r, c = i[:, None], i[None, :]
    same = (r // CH) == (c // CH)
    out = np.zeros((NCONST, P, P), np.float32)
    out[IDENT] = r == c
    out[UPPER] = same & (r <= c)
    out[BLOCK] = same
    out[STRICT] = same & (r < c)
    out[PAIR] = -1.0 * ((r // 2 == c // 2) & (r > c))
    out[PAIR_T] = out[PAIR].T
    for n, level in enumerate(LEVELS):
        size = 2 ** level
        out[LEVEL2 + n] = (r // size == c // size) & (r // (size // 2) != c // (size // 2)) & (r > c)
    out[ROWS_A] = (r < CH) & (c >= 0)
    out[ROWS_B] = (r >= CH) & (c >= 0)
    return np.ascontiguousarray(out.transpose(1, 0, 2))


SEMAPHORES = """
c_load v_load x_load0 x_load1 wba_load row_load vec_ps cT_ps cT_e cT cw_hi cw x_ss x_e x_n xt_ps xt ada_row ada_cps ada_col
h_full h_hi h_lo wba_hi wba_lo ba_ps baT ba_turn ba_sb g_e1 g_e2 g_e3 g_g cum_ps cum_sb cum_d gates zeroed
hi lo used act_link dve_link
cin_ready conv_done exp_a act_ready bss tails nat_ps nat_a sq_a ss_a x_a y_a scal_a knb_a pool_a gbc tr_a tra_act kbt
grow_ps diff et em mt_ps mt at_ps at m_ps m bm st0 lx_ps lx ly_ps ly lt_ps lt w_ps w_sb u_ps u_sb
sa_ps vn sb_ps so ss_new s_load s_zero s_out sq_o x_o y_o on_o o_ps oa ga_z ga_e sga
bz bnat_ps bnat bsq x_b y_b bk_y bkw bqn cache_load ct_ps ct bias_load bias btr_ps btr
qk sadd smax pexp pn pt_ps pt pv ob gb_z gb_e sgb k_out v_out cs_ps cs_sb cs_out
o_hi o_lo m_e m_sig mrg_a mrg m_hi m_lo f_g f_ps f_sb x_tail0 x_tail1 y_out0 y_out1
""".split()


class Link:

    def __init__(self, eng, sem):
        self.eng, self.sem, self.n, self.extra, self.start = eng, sem, 0, 0, 0

    def __call__(self, ins):
        self.n += 1
        ins.then_inc(self.sem, 1)
        self.eng.wait_ge(self.sem, self.n + self.extra)

    def loop(self, i, first, per):
        self.start, self.extra, self.per = self.n, (i - first) * per, per

    def end(self, times):
        assert self.n - self.start == self.per, (self.n - self.start, self.per)
        self.n, self.extra = self.start + self.per * times, 0


def again(h):
    return not (isinstance(h, int) and h == 0)


def is_last(j):
    return isinstance(j, int) and j == KT - 1


def hybrid_layer(nc, io):
    ctx = ExitStack()
    with ctx:
        def sb(name, shape, dt=F32, where=ctx):
            return where.enter_context(nc.sbuf_tensor(name, shape, dt))

        s = {n: ctx.enter_context(nc.semaphore(n)) for n in SEMAPHORES}
        x_tail = [s["x_tail0"], s["x_tail1"]]
        y_out = [s["y_out0"], s["y_out1"]]
        landed = [ctx.enter_context(nc.semaphore(f"landed{r}")) for r in range(RING_START)]

        ps = ctx.enter_context(nc.psum_tensor("ps", [P, 8, 512], F32))
        G1, G2, A1, A2 = 4, 5, 6, 7

        Hh = sb("Hh", [P, KT, N], F32R)
        Hl = sb("Hl", [P, KT, N], F32R)
        Of = sb("Of", [P, KT, N])
        raw = sb("raw", [P, RING, SLOT])
        whi = sb("whi", [P, RING, SLOT], F32R)
        wlo = sb("wlo", [P, RING, SLOT], F32R)
        eye = sb("eye", [P, P])
        modT = sb("modT", [P, 3 * KT, 2])
        vecT = sb("vecT", [P, 2, P])
        cw = sb("cw", [P, 4 * KT + P - 4], F32R)
        cvs = sb("cvs", [P, KT, 2])
        conv_cols = vecT[:, 0, 0:96].rearrange("p (i b) -> p b i", i=4)
        norm_col = vecT[:, 0, 96:112]
        gnw_col = vecT[:, 0, 112:113]
        qnw_col = vecT[:, 0, 113:114]
        state_cols = vecT[:, 1, 0:72].rearrange("p (i b) -> p b i", i=3)
        adab_cols = vecT[:, 1, 72:120]

        NG = HEADS * (NT + 1)
        gsz = [P, HEADS, NT + 1]
        beta, gg, Gc, eG, egl = (sb(n, gsz) for n in ("beta", "gg", "Gc", "eG", "egl"))
        glb = sb("glb", [P, 2, HEADS, NT + 1])
        cs = sb("cs", [P, 6, 24])

        masks = ExitStack()
        con = sb("con", [P, NCONST, P], where=masks)

        begin = ExitStack()
        xT = sb("xT", [P, KT, N], where=begin)
        xn = [sb(f"xn{i}", [P, D], where=begin) for i in range(2)]
        cv = sb("cv", [P, KT, 2], where=begin)

        mrow = sb("mrow", [4, SLOT], where=begin)
        vrow = sb("vrow", [P, 2, P], where=begin)
        crow = sb("crow", [2 * KT, P], where=begin)
        ce = sb("ce", [P, 2 * KT], where=begin)
        xs = sb("xs", [P, 8], where=begin)
        hA = sb("hA", [P, KT, 2], where=begin)
        whi_more = sb("whi_more", [P, RING_PARTS - RING, SLOT], F32R, where=begin)
        wlo_more = sb("wlo_more", [P, RING_PARTS - RING, SLOT], F32R, where=begin)
        fold = sb("fold", [4, 2], where=begin)
        wba = sb("wba", [P, KT, 16], where=begin)
        wbs = sb("wbs", [P, 32 * KT + P - 32], F32R, where=begin)
        baT = sb("baT", [32, N], where=begin)
        bar = sb("bar", [P, NT + 1, 32], where=begin)
        bax = sb("bax", [P, 2 * HEADS, NT + 1], where=begin)
        dtb = sb("dtb", [P, 2, HEADS], where=begin)
        gt = [sb(f"gt{i}", gsz, where=begin) for i in range(6)]
        begin.close()

        heads = ExitStack()
        def nat(name):
            return sb(name, [P, NT + 1, P], where=heads)
        cin = sb("cin", [P, 3 + N + 3], where=heads)
        cacc = sb("cacc", [P, N + 3], where=heads)
        eT = sb("eT", [P, N + 3], where=heads)
        aT = sb("aT", [P, N], where=heads)
        q_nat, k_nat, v_nat, sqb, Mn, B0, B1, MT, AT, Sm, Tm, Xs, vb, kbg, kg = (nat(n) for n in (
            "q_nat", "k_nat", "v_nat", "sqb", "Mn", "B0", "B1", "MT", "AT", "Sm", "Tm", "Xs", "vb", "kbg", "kg"))
        kn, kb, qn, qg, U_, o_nat, ET, EU, ES, gbc = Mn, B0, B1, MT, MT, v_nat, sqb, Sm, Tm, Xs
        knT = sb("knT", [P, N], where=heads)
        kbT = sb("kbT", [P, N], where=heads)
        qnT = sb("qnT", [P, N], where=heads)
        qgw = sb("qgw", [P, (NCH + 1) * P], where=heads)
        Vn = sb("Vn", [P, P], where=heads)
        Vs = sb("Vs", [NS, P], where=heads)
        St = sb("St", [P, P], where=heads)
        Ss = sb("Ss", [P, P], where=heads)
        sga = sb("sga", [P, N], where=heads)
        sgb = sb("sgb", [P, N], where=heads)
        bv = nat("bv")
        kc = sb("kc", [P, 2, P], where=heads)
        vc = sb("vc", [P, 2, P], where=heads)
        kcT = sb("kcT", [P, PAST], where=heads)
        Bp = sb("Bp", [P, 2 * P], where=heads)
        kwb = sb("kwb", [P, P], where=heads)
        st = sb("st", [P, 16, 5], where=heads)
        sm = sb("sm", [P, 2, 4], where=heads)
        heads.close()
        bq, bk = q_nat, k_nat
        kT, qT, PT = knT, qnT, kbT
        Pb = [Xs, B0]
        csT = cacc[:, 0:2 * P].rearrange("p (a n) -> p a n", a=2)
        mrows = [mrow, eT[0:2, 0:SLOT]]
        raw_start = Of[:, :, :].rearrange("p k n -> p (k n)")[:, 0:RING_START * SLOT].rearrange("p (r n) -> p r n", n=SLOT)

        cw4 = cw[:, 0:4 * KT].rearrange("p (k c) -> p k c", c=4)
        wbs2 = wbs[:, 0:32 * KT].rearrange("p (k a n) -> p k a n", a=2, n=16)
        (SS_Q, SS_K, X_Q, X_K, Y_Q, Y_K, T_Q, T_K, SC_Q, SC_QG, SC_KB, SC_KBG, SC_KG) = range(13)

        masks.close()
        late = ExitStack()
        Oh = sb("Oh", [P, KT, N], F32R, where=late)
        Ol = sb("Ol", [P, KT, N], F32R, where=late)
        sg = [sb(f"sg{i}", [P, N], where=late) for i in range(2)]
        tmp = sb("tmp", [P, N], where=late)
        late.close()
        last = ExitStack()
        fo = sb("fo", [P, 2, N], where=last)
        xr = sb("xr", [P, 2, NT + 1, P], where=last)
        yo = sb("yo", [P, 2, NT + 1, P], where=last)
        last.close()

        w_in = io["w_in"].rearrange("o d n -> (o d) n")
        ada_w = io["ada_w"].rearrange("o d n -> (o d) n")
        wpa = io["w_proj_a"].rearrange("o d n -> (o d) n")
        wpb = io["w_proj_b"].rearrange("o d n -> (o d) n")
        w_out = io["w_out"].rearrange("o d n -> (o d) n")
        x_p = io["x_prompt"].rearrange("b t d -> (b t) d")
        x_s = io["x_sample"].rearrange("b t d -> (b t) d")
        y_p = io["y_prompt"].rearrange("b t d -> (b t) d")
        y_s = io["y_sample"].rearrange("b t d -> (b t) d")
        sdelta = io["state_delta"].rearrange("o b h k v -> (o b h) k v")
        pdel_o = io["p_delta"].rearrange("o b h k v -> (o b h) k v")
        sdel_o = io["s_delta"].rearrange("o b h k v -> (o b h) k v")
        ck = io["cache_k"].rearrange("o b t h d -> h (o b t) d")
        cvd = io["cache_v"].rearrange("o b t h d -> h (o b t) d")
        kv_o = {n: io[n].rearrange("o b t h d -> h (o b t) d") for n in ("p_k", "p_v", "s_k", "s_v")}
        relx = io["rel_ext"]

        def blocks_of(w, row0, col0, count=4):
            return w[row0:row0 + count * P, bass.ds(col0, P)].rearrange("(a p) n -> p a n", p=P)

        def split4(ap):
            return ap.rearrange("p (a n) -> p a n", a=4)

        def rows_of(i):
            return P if i < NT else NS

        def junk_rows(rows):
            return Hl[0:rows, 0:4, 0:D // 4]

        H_PLACES = {(5, 2 * k + 1): k for k in range(8)}
        H_PLACES.update({(6, 8 + 2 * k): 8 + k for k in range(4)})

        def bank(b, cols=512):
            return ps[:, b, 0:cols]

        def tiles(b):
            return ps[:, b, :].rearrange("p (t n) -> p t n", t=4)

        def acc(pair):
            return ps[:, 2 * pair:2 * pair + 2, 0:HALF]

        def halves(ap):
            return ap.rearrange("p (a n) -> p a n", a=2)

        def wide(cols):
            return cols.unsqueeze(2).to_broadcast([cols.shape[0], cols.shape[1], P])

        block = ctx.enter_context(nc.Block())

        SL_HEAD = 8 * KT
        SL_GATE = SL_HEAD + 32 * HEADS
        SL_MERGE = SL_GATE + 4 * KT
        SL_OUT = SL_MERGE + 12 * KT
        LANDED_START = 16 * SL_HEAD // RING_START
        SPLIT_MERGE = SL_MERGE - 4 * KT
        SPLIT_OUT = SL_OUT - 4 * KT

        @block.sync
        def _(sp):
            def ada_slot(c, k, col):
                r = k % RING_START
                if not (isinstance(c, int) and c == 0 and k < RING_START):
                    sp.wait_ge(s["lo"], c * KT + (k - RING_START + 1))
                sp.dma_start(raw_start[:, r, :], ada_w[k * P:(k + 1) * P, bass.ds(col, SLOT)]).then_inc(landed[r], 16)

            def slot(n, r, src):
                sp.wait_ge(s["lo"], n - RING + 1)
                sp.dma_start(split4(raw[:, r, :]), src).then_inc(landed[r], 16)

            for c in range(2):
                for k in range(KT):
                    ada_slot(c, k, D * (1 - c))
            with sp.Fori(0, 3) as i:
                for half in range(2):
                    for k in range(KT):
                        ada_slot(i * 2 + 2 + half, k, i * SLOT + (SLOT + D * (1 - half)))

            unit_cols = [0, QK, 2 * QK, 3 * QK, COL_B, COL_B + QK, COL_B + 2 * QK, COL_B + 3 * QK]

            def head_slots(h, first):
                for u, col in enumerate(unit_cols):
                    for k4 in range(4):
                        c = 4 * u + k4
                        src = blocks_of(w_in, 512 * k4, h * P + col)
                        if first and c < RING:
                            sp.wait_ge(s["lo"], SL_HEAD - RING_START + c + 1)
                            sp.dma_start(split4(raw[:, c, :]), src).then_inc(landed[c], 16)
                        else:
                            slot(h * 32 + (SL_HEAD + c), c % RING, src)

            head_slots(0, True)
            with sp.Fori(1, HEADS) as h:
                head_slots(h, False)
            for c in range(4):
                for k in range(KT):
                    n = SL_GATE + KT * c + k
                    sp.wait_ge(s["lo" if n < SL_GATE + RING else "used"], n - RING + 1)
                    sp.dma_start(raw[:, k % RING, :], ada_w[k * P:(k + 1) * P, 2 * D + c * SLOT:2 * D + (c + 1) * SLOT]).then_inc(landed[k % RING], 16)

            def merge_slots(i, first):
                for c in range(12):
                    if c < 8:
                        src = blocks_of(w_in, 512 * (c % 4), i * P + (COL_M - P + D * (c // 4)))
                    else:
                        src = blocks_of(wpa if c < 10 else wpb, 512 * (c % 2), i * P - P)
                    if first and c < RING:
                        sp.wait_ge(s["used"], SL_MERGE + c - RING + 1)
                        sp.dma_start(split4(raw[:, c, :]), src).then_inc(landed[c], 16)
                    else:
                        slot(i * 12 + (SPLIT_MERGE - 12 + c), c % RING, src)
            merge_slots(1, True)
            with sp.Fori(2, KT + 1) as i:
                merge_slots(i, False)
            with sp.Fori(0, KT) as j:
                for c in range(4):
                    slot(j * 4 + SPLIT_OUT + c, c, blocks_of(w_out, 512 * c, j * P))

        def start_parts(n):
            r = n % RING_PARTS
            return (whi[:, r, :], wlo[:, r, :]) if r < RING else (whi_more[:, r - RING, :], wlo_more[:, r - RING, :])

        def start_hi(act, n):
            act.wait_ge(landed[n % RING_START], 16 * (n // RING_START + 1))
            if n >= RING_PARTS:
                act.wait_ge(s["used"], n - RING_PARTS + 1)
            act.activation(start_parts(n)[0], raw_start[:, n % RING_START, :], ACT.Copy).then_inc(s["hi"], 1)

        def start_lo(dve, n):
            dve.wait_ge(s["hi"], n + 1)
            high, low = start_parts(n)
            dve.tensor_tensor(low, raw_start[:, n % RING_START, :], high.bitcast(F32), ALU.subtract).then_inc(s["lo"], 1)

        def split_hi(act, base, c):
            r = c % RING
            act.wait_ge(landed[r], base * (16 // RING) + ((c - r - SL_HEAD) * (16 // RING) + 16 + LANDED_START))
            src = raw[:, r, :]
            if isinstance(base, int) and base == SL_HEAD and c < RING:
                act.wait_ge(s["used"], max(m for m in range(SL_HEAD) if m % RING_PARTS == r) + 1)
            if not (isinstance(base, int) and base + c < RING):
                act.wait_ge(s["used"], base + (c - RING + 1))
            act.activation(whi[:, r, :], src, ACT.Copy).then_inc(s["hi"], 1)

        def split_lo(dve, base, c):
            r = c % RING
            dve.wait_ge(s["hi"], base + (c + 1))
            dve.tensor_tensor(wlo[:, r, :], raw[:, r, :], whi[:, r, :].bitcast(F32), ALU.subtract).then_inc(s["lo"], 1)

        def rsqrt_newton(link, dve, y, x, t):
            link(dve.tensor_tensor(t, y, y, ALU.mult))
            link(dve.tensor_tensor(t, t, x, ALU.mult))
            link(dve.tensor_scalar(t, t, -0.5, 1.5, ALU.mult, ALU.add))
            link(dve.tensor_tensor(y, y, t, ALU.mult))

        def run_head(steps, h, place):
            for at, step in steps:
                if at == place + GRID and again(h):
                    step(h - 1)
            for at, step in steps:
                if at == place:
                    step(h)

        def run_tail(steps, place):
            for at, step in steps:
                if at == place + GRID:
                    step(HEADS - 1)

        @block.scalar
        def _(act):
            link = Link(act, s["act_link"])
            act.add_instruction(mybir.InstLoadActFuncSet(name=nc.get_next_instruction_name(), act_func_set_id=EXP_LN_SET, engine=mybir.EngineType.Activation))

            def a_evac(i):
                def go(h):
                    pair = i % 2
                    act.wait_ge(s["used"], h * 32 + (SL_HEAD + 4 * (i + 1)))
                    if not again(h):
                        act.wait_ge(s["zeroed"], 1)
                    if i or again(h):
                        act.wait_ge(s["conv_done"], h * 3 + i)
                        act.wait_ge(s["tails"], h * 3 + i)
                    act.copy(cin[:, 3:3 + HALF], ps[:, 2 * pair, 0:HALF])
                    act.copy(cin[:, 3 + HALF:3 + NP], ps[:, 2 * pair + 1, 0:NP - HALF])
                    act.copy(cin[:, 6 + NP:6 + N], ps[:, 2 * pair + 1, NP - HALF:HALF])
                    act.copy(cin[:, 3 + NP:6 + NP], state_cols[:, h + 8 * i, :]).then_inc(s["cin_ready"], 1)
                return go

            def a_exp(i):
                def go(h):
                    act.wait_ge(s["conv_done"], h * 3 + i + 1)
                    if i == 0 and again(h):
                        act.wait_ge(s["sgb"], h)
                    act.activation(eT[:, :], cacc[:, :], ACT.Exp, scale=-1.0).then_inc(s["exp_a"], 1)
                return go

            def evac_nat(ps_sem, sb_sem, dst, count, bank_a):
                def go(h):
                    act.wait_ge(s[ps_sem], h * 3 + count)
                    act.copy(dst[:, 0:NT, :], tiles(bank_a))
                    act.copy(dst[0:NS, NT, :], ps[0:NS, bank_a + 1, 0:P]).then_inc(s[sb_sem], 1)
                return go

            def a_nat(i):
                def go(h):
                    if again(h) and i < 2:
                        act.wait_ge(s["bqn" if i == 0 else "btr_ps"], h if i == 0 else 2 * h)
                        act.wait_ge(s["bnat_ps"], 3 * h)
                        if i == 1:
                            act.wait_ge(s["k_out"], 32 * h)
                    if again(h) and i == 2:
                        act.wait_ge(s["o_ps"], h)
                    evac_nat("nat_ps", "nat_a", (q_nat, k_nat, v_nat)[i], i + 1, G1 if i < 2 else A1)(h)
                return go

            def a_lnexp(x_sem, y_sem, lo, n):
                def go(h):
                    act.wait_ge(s[x_sem], h + 1)
                    link(act.activation(st[:, T_Q:T_Q + n, :], st[:, X_Q:X_Q + n, :], ACT.Ln))
                    act.activation(st[:, Y_Q:Y_Q + n, :], st[:, T_Q:T_Q + n, :], ACT.Exp, scale=-0.5).then_inc(s[y_sem], 1)
                return go

            def a_trev(dst, n):
                def go(h):
                    act.wait_ge(s["tr_a"], h * 4 + (1, 3, 4)[n])
                    if n < 2:
                        act.copy(dst[:, 0:NP], bank(G1))
                        act.copy(dst[:, NP:N], ps[:, G2, 0:NS]).then_inc(s["tra_act"], 1)
                    else:
                        act.copy(qgw[:, CH:CH + 4 * 256].rearrange("p (t n) -> p t n", n=256)[:, :, 0:P], tiles(G1))
                        act.copy(qgw[:, NCH * P + NS:NCH * P + 2 * NS], ps[:, G2, 0:NS]).then_inc(s["tra_act"], 1)
                return go

            def a_et(h):
                act.wait_ge(s["diff"], h + 1)
                act.activation(ET[:, 0:NT, :], ET[:, 0:NT, :], ACT.Exp)
                act.activation(ET[0:NS, NT, 0:NS], ET[0:NS, NT, 0:NS], ACT.Exp).then_inc(s["et"], 1)

            def a_m(h):
                act.wait_ge(s["m_ps"], h + 1)
                act.copy(Mn[:, 0:NT, :], tiles(G1))
                act.copy(Mn[0:NS, NT, 0:NS], ps[0:NS, G2, 0:NS]).then_inc(s["m"], 1)

            def level_evac(ps_sem, sb_sem, dst, per, n):
                def go(h):
                    act.wait_ge(s[ps_sem], h * per + n + 1)
                    act.copy(dst[:, 0:NT, :], tiles(G1))
                    act.copy(dst[0:NS, NT, 0:NS], ps[0:NS, G2, 0:NS]).then_inc(s[sb_sem], 1)
                return go

            def a_w(h):
                act.wait_ge(s["w_ps"], h + 1)
                for a in range(2):
                    act.copy(qgw[:, 0:NCH * P].rearrange("p (t n) -> p t n", n=256)[:, :, 192 * a:192 * a + CH],
                             tiles(G1)[:, :, CH * a:CH * a + CH])
                act.copy(qgw[:, NCH * P:NCH * P + NS], ps[:, G2, 0:NS]).then_inc(s["w_sb"], 1)

            def a_o(n):
                def go(h):
                    act.wait_ge(s["sb_ps"], h * 9 + max(n, 1) + 1)
                    if n == 0:
                        ins = act.copy(o_nat[0:NS, NT, :], ps[NS:2 * NS, G1, P:2 * P])
                    else:
                        c = n - 1
                        r0 = CH * (c % 2)
                        ins = act.copy(o_nat[r0:r0 + CH, c // 2, :], ps[CH - r0:2 * CH - r0, G1, 0:P])
                    ins.then_inc(s["so"], 1)
                return go

            def gate_evac(u, z, sem):
                def go(h):
                    act.wait_ge(s["used"], h * 32 + (SL_HEAD + 4 * (u + 1)))
                    if again(h):
                        act.wait_ge(s["oa" if u == 3 else "ob"], h if u == 3 else 5 * h)
                    act.copy(halves(z[:, :]), acc(1)).then_inc(s[sem], 1)
                return go

            def gate_exp(z, z_sem, sem):
                def go(h):
                    act.wait_ge(s[z_sem], h + 1)
                    if z is sga:
                        act.wait_ge(s["act_ready"], h * 3 + 3)
                    else:
                        act.wait_ge(s["sga"], h + 1)
                    act.activation(eT[:, 0:N], z[:, :], ACT.Exp, scale=-1.0).then_inc(s[sem], 1)
                return go

            def b_evac(i):
                def go(h):
                    pair = i % 2
                    act.wait_ge(s["used"], h * 32 + (SL_HEAD + 4 * (5 + i)))
                    if i == 0:
                        act.wait_ge(s["nat_ps"], h * 3 + 3)
                    else:
                        act.wait_ge(s["bnat_ps"], h * 3 + i)
                    act.copy(halves(aT[:, :]), acc(pair)).then_inc(s["bz"], 1)
                return go

            def b_nat(i):
                def go(h):
                    if i == 0:
                        act.wait_ge(s["pool_a"], h * 5 + 2)
                    if i == 1:
                        act.wait_ge(s["pool_a"], h * 5 + 5)
                    if i == 2 and again(h):
                        act.wait_ge(s["pv"], 5 * h)
                        act.wait_ge(s["v_out"], 32 * h)
                    evac_nat("bnat_ps", "bnat", (bq, bk, bv)[i], i + 1, A1)(h)
                return go

            def b_ct(h):
                act.wait_ge(s["ct_ps"], h + 1)
                act.copy(kcT[:, :], ps[:, A1, 0:PAST]).then_inc(s["ct"], 1)

            def b_trev(n):
                def go(h):
                    act.wait_ge(s["btr_ps"], h * 2 + n + 1)
                    act.wait_ge(s["at_ps"], h + 1)
                    dst = (kT, qT)[n]
                    if n == 0:
                        act.copy(dst[:, 0:NP], bank(A1))
                        act.copy(dst[:, NP:N], ps[:, A2, 0:NS]).then_inc(s["btr"], 1)
                    else:
                        act.activation(dst[:, 0:NP], bank(A1), ACT.Copy, scale=qnw_col)
                        act.activation(dst[:, NP:N], ps[:, A2, 0:NS], ACT.Copy, scale=qnw_col).then_inc(s["btr"], 1)
                return go

            def key_count(i):
                return (i + 1) * P if i < NT else PAST + NS

            def b_exp(i):
                def go(h):
                    rows = P if i < NT else NS
                    n = key_count(i)
                    act.wait_ge(s["smax"], h * 5 + i + 1)
                    p = Pb[i % 2][0:rows, :, :].rearrange("p a n -> p (a n)")[:, 0:n]
                    act.activation(p, p, ACT.Exp, bias=sm[0:rows, i % 2, 0:1], accum_out=sm[0:rows, i % 2, 1:2]).then_inc(s["pexp"], 1)
                return go

            def b_pt(i):
                def go(h):
                    act.wait_ge(s["pt_ps"], h * 5 + i + 1)
                    if i == 0:
                        act.wait_ge(s["mt_ps"], h + 1)
                    else:
                        act.wait_ge(s["pv"], h * 5 + i)
                    if i < NT:
                        n = (i + 1) * P
                        act.copy(PT[:, 0:n], ps[:, A2, 0:n]).then_inc(s["pt"], 1)
                    else:
                        act.copy(PT[:, 0:2 * NS], ps[:, A2, 0:2 * NS])
                        act.copy(PT[0:NS, 2 * NS:3 * NS], ps[0:NS, A2, 2 * NS:3 * NS]).then_inc(s["pt"], 1)
                return go

            def head_loads(h):
                if again(h):
                    act.wait_ge(s["pv"], 5 * h)
                    act.wait_ge(s["s_out"], 32 * h)
                    act.wait_ge(s["ob"], 5 * h)
                act.dma_start(kc[:, :, :], ck[h, :, :].rearrange("(a p) d -> p a d", p=P)).then_inc(s["cache_load"], 16)
                act.dma_start(vc[:, :, :], cvd[h, :, :].rearrange("(a p) d -> p a d", p=P)).then_inc(s["cache_load"], 16)
                act.dma_start(Ss[:, :], sdelta[h, :, :]).then_inc(s["s_load"], 16)
                rows = relx[h, :]
                act.dma_start(Bp[:, :], bass.AP(rows.tensor, rows.offset, [[1, P], [1, 2 * P]])).then_inc(s["bias_load"], 16)

            def k_store(h):
                act.wait_ge(s["bkw"], h + 1)
                act.dma_start(kv_o["p_k"][h, :, :].rearrange("(t p) d -> p t d", p=P), bk[:, 0:NT, :]).then_inc(s["k_out"], 16)
                act.dma_start(kv_o["s_k"][h, :, :], bk[0:NS, NT, :]).then_inc(s["k_out"], 16)

            def v_store(h):
                act.wait_ge(s["bnat"], h * 3 + 3)
                act.dma_start(kv_o["p_v"][h, :, :].rearrange("(t p) d -> p t d", p=P), bv[:, 0:NT, :]).then_inc(s["v_out"], 16)
                act.dma_start(kv_o["s_v"][h, :, :], bv[0:NS, NT, :]).then_inc(s["v_out"], 16)

            def s_store(h):
                act.wait_ge(s["ss_new"], h * 9 + 9)
                act.dma_start(pdel_o[h, :, :], St[:, :]).then_inc(s["s_out"], 16)
                act.dma_start(sdel_o[h, :, :], Ss[:, :]).then_inc(s["s_out"], 16)

            def kb_t(h):
                act.wait_ge(s["tr_a"], h * 4 + 2)
                act.copy(kbT[:, 0:NP], bank(G1))
                act.copy(kbT[:, NP:N], ps[:, G2, 0:NS]).then_inc(s["kbt"], 1)

            def u_evac(h):
                act.wait_ge(s["u_ps"], h + 1)
                act.copy(U_[:, 0:NT, :], tiles(G1))
                act.copy(U_[0:NS, NT, :], ps[0:NS, G2, 0:P]).then_inc(s["u_sb"], 1)

            steps = [(68 + 4 * i + max(i - 2, 0), b_pt(i)) for i in range(5)]
            steps += [(32, kb_t), (56, u_evac), (8, a_evac(0)), (16, a_evac(1)), (24, a_evac(2)), (11, a_exp(0)), (18, a_exp(1)), (34, a_exp(2)),
                     (19, a_nat(0)), (24, a_nat(1)), (27, a_lnexp("x_a", "y_a", 0, 2)), (28, a_et),
                     (31, a_trev(knT, 0)), (44, a_nat(2)), (32, gate_evac(3, sga, "ga_z")), (45, gate_exp(sga, "ga_z", "ga_e")), (33, a_trev(qnT, 1)),
                     (34, a_trev(None, 2)), (37, a_m), (55, a_w)]
            for n in range(5):
                steps.append((40 + 3 * n, level_evac("lx_ps", "lx", Xs, 5, n)))
                if n < 4:
                    steps.append((42 + 3 * n, level_evac("lt_ps", "lt", Tm, 4, n)))
            steps += [(59 + 2 * max(n - 1, 0), a_o(n)) for n in range(9)]
            steps += [(76, a_lnexp("x_o", "y_o", 0, 1))]
            steps += [(45, b_evac(0)), (48, b_evac(1)), (56, b_evac(2)), (47, b_nat(0)), (52, b_nat(1)), (59, b_nat(2)),
                      (49, b_ct), (54, a_lnexp("x_b", "y_b", 0, 2)), (58, b_trev(0)), (60, b_trev(1)),
                      (GRID, gate_evac(7, sgb, "gb_z")), (GRID, gate_exp(sgb, "gb_z", "gb_e")), (26, head_loads), (60, k_store), (61, v_store), (76, s_store)]
            steps += [(64 + 4 * i, b_exp(i)) for i in range(5)]
            steps.sort(key=lambda x: x[0])

            act.dma_start(eye[:, :], io["con"][:, IDENT, :]).then_inc(s["c_load"], 16)
            act.dma_start(crow[0:KT, :], io["c_prompt"].rearrange("b (t d) -> (b t) d", d=P)).then_inc(s["c_load"], 16)
            act.dma_start(crow[KT:2 * KT, :], io["c_sample"].rearrange("b (t d) -> (b t) d", d=P)).then_inc(s["c_load"], 16)

            def x_in(t):
                if t < NT:
                    act.dma_start(xn[t % 2][:, :], x_p[t * P:(t + 1) * P, :]).then_inc(s[f"x_load{t % 2}"], 16)
                else:
                    act.dma_start(xn[t % 2][0:NS, :], x_s).then_inc(s[f"x_load{t % 2}"], 16)
            x_in(0)
            x_in(1)
            for n in range(LEAD_START):
                start_hi(act, n)
            act.wait_ge(s["cT_ps"], 1)
            act.copy(cv[:, :, :].rearrange("p k g -> p g k"), ps[:, G2, 0:2 * KT].rearrange("p (g k) -> p g k", g=2))
            act.activation(ce[:, :], ps[:, G2, 0:2 * KT], ACT.Exp, scale=-1.0).then_inc(s["cT_e"], 1)
            act.wait_ge(s["cT"], 1)
            act.activation(cw4[:, :, 0:2], cvs[:, :, :], ACT.Copy).then_inc(s["cw_hi"], 1)

            def x_work(t, k):
                rows = rows_of(t)
                if k == 1:
                    act.wait_ge(s[f"x_load{t % 2}"], 16 * (t // 2 + 1))
                    act.activation(junk_rows(rows), split4(xn[t % 2][0:rows, :]), ACT.Square, accum_out=xs[0:rows, 0:1]).then_inc(s["x_ss"], 1)
                if k == 3:
                    act.wait_ge(s["x_e"], 2 * t + 1)
                    link(act.activation(xs[0:rows, 2:3], xs[0:rows, 1:2], ACT.Ln))
                    act.activation(xs[0:rows, 3:4], xs[0:rows, 2:3], ACT.Exp, scale=-0.5).then_inc(s["x_e"], 1)
                if k in (9, 11, 13, 15):
                    q = (k - 9) // 2
                    act.wait_ge(s["xt_ps"], 4 * t + q + 1)
                    out = xT[:, 4 * q:4 * q + 4, t * P:t * P + rows]
                    act.copy(out, tiles(G1 + q % 2)[:, :, 0:rows]).then_inc(s["xt"], 1)
                if k == 15 and t + 2 <= NT:
                    x_in(t + 2)

            def h_high(k):
                act.wait_ge(s["h_full"], k + 1)
                act.activation(Hh[:, k, :], xT[:, k, :], ACT.Copy).then_inc(s["h_hi"], 1)

            for c in range(8):
                for k in range(KT):
                    n = KT * c + k + LEAD_START
                    if n < SL_HEAD:
                        start_hi(act, n)
                    elif n < SL_HEAD + LEAD:
                        split_hi(act, SL_HEAD, n - SL_HEAD)
                    if c <= NT:
                        x_work(c, k)
                    if (c, k) == (1, 0):
                        act.wait_ge(s["vec_ps"], 1)
                        act.copy(vecT[:, 0, 0:114], ps[:, A1, 0:114])
                        act.copy(vecT[:, 1, 0:120], ps[:, A1, P:P + 120])
                    if (c, k) in H_PLACES:
                        h_high(H_PLACES[c, k])
                    if c == 5 and k == 15:
                        act.wait_ge(s["wba_load"], 16)
                        act.activation(wbs2[:, :, 0, :], wba[:, :, :], ACT.Copy).then_inc(s["wba_hi"], 1)
            for k in range(12, KT):
                h_high(k)

            def beta_rows(h):
                act.wait_ge(s["ba_ps"], 1)
                act.copy(halves(baT[:, :]), ps[0:32, G1:G1 + 2, 0:HALF]).then_inc(s["baT"], 1)

            def beta_nat(h):
                act.wait_ge(s["ba_turn"], 1)
                act.copy(bar[:, 0:NT, :], ps[:, A1, 0:32 * NT].rearrange("p (t n) -> p t n", n=32))
                act.copy(bar[0:NS, NT, :], ps[0:NS, A1, 32 * NT:32 * NT + 32]).then_inc(s["ba_sb"], 1)

            def gate_exps(h):
                act.wait_ge(s["g_e1"], 1)
                link(act.activation(gt[0][:, :, :], bax[:, 0:HEADS, :], ACT.Exp, scale=-1.0))
                act.activation(gt[2][:, :, :], gt[1][:, :, :], ACT.Exp, scale=-1.0)
                act.activation(dtb[:, 1, :], dtb[:, 1, :], ACT.Exp).then_inc(s["g_e2"], 1)

            def gate_ln(h):
                act.wait_ge(s["g_e1"], 2)
                act.activation(gt[4][:, :, :], gt[3][:, :, :], ACT.Ln).then_inc(s["g_e3"], 1)

            def gate_sums(h):
                act.wait_ge(s["cum_ps"], 1)
                act.copy(Gc[:, :, :], ps[:, G2, 0:NG].rearrange("p (h t) -> p h t", h=HEADS))
                act.activation(eG[:, :, :], ps[:, G2, 0:NG].rearrange("p (h t) -> p h t", h=HEADS), ACT.Exp)
                act.copy(gt[0][:, :, :], ps[:, G2, NG:2 * NG].rearrange("p (h t) -> p h t", h=HEADS))
                act.activation(glb[:, :, :, :], ps[:, G2, 2 * NG:4 * NG].rearrange("p (a h t) -> p a h t", a=2, h=HEADS), ACT.Exp).then_inc(s["cum_sb"], 1)

            def gate_last(h):
                act.wait_ge(s["cum_d"], 1)
                act.activation(egl[:, :, :], gt[1][:, :, :], ACT.Exp).then_inc(s["gates"], 1)

            def body(h, last=False):
                for place in range(GRID):
                    if place % 2 == 0 and not (last and place // 2 + LEAD >= 32):
                        split_hi(act, h * 32 + SL_HEAD, place // 2 + LEAD)
                    if not again(h):
                        run_head([(9, beta_rows), (10, beta_nat), (11, gate_exps), (12, gate_ln), (14, gate_sums), (15, gate_last)], h, place)
                    run_head(steps, h, place)
            body(0)
            with act.Fori(1, HEADS - 1) as h:
                link.loop(h, 1, ACT_LINKS)
                body(h)
            link.end(HEADS - 2)
            body(HEADS - 1, True)

            for place in range(32):
                run_tail(steps, place)
            for c in range(LEAD):
                split_hi(act, SL_MERGE, c)
            act.wait_ge(s["cs_ps"], 1)
            act.copy(csT[:, 0, :], ps[:, A1, 0:P])
            act.copy(csT[0:16, 1, :], ps[0:16, A1, P:2 * P]).then_inc(s["cs_sb"], 1)
            act.wait_ge(s["cs_sb"], 1)
            pc = io["p_conv"].rearrange("o b i (c d) -> (o b i c) d", d=P)
            sc = io["s_conv"].rearrange("o b i (c d) -> (o b i c) d", d=P)
            act.dma_start(pc, csT[0:72, 0, :]).then_inc(s["cs_out"], 16)
            act.dma_start(sc[0:P - 72, :], csT[72:P, 0, :]).then_inc(s["cs_out"], 16)
            act.dma_start(sc[P - 72:72, :], csT[0:16, 1, :]).then_inc(s["cs_out"], 16)
            def branches_high(place):
                if place == 3:
                    act.wait_ge(s["oa"], HEADS)
                    act.wait_ge(s["ob"], 5 * HEADS)
                    act.wait_ge(s["s_out"], 32 * HEADS)
                    act.wait_ge(s["k_out"], 32 * HEADS)
                    act.wait_ge(s["v_out"], 32 * HEADS)
                    act.wait_ge(s["cs_out"], 16 * 3)
                    act.wait_ge(s["ada_cps"], 12)
                if 3 <= place < 3 + KT // 2:
                    for k in (2 * (place - 3), 2 * (place - 3) + 1):
                        act.activation(Oh[:, k, :], Of[:, k, :], ACT.Copy).then_inc(s["o_hi"], 1)

            def merged_high(k):
                act.wait_ge(s["used"], SL_OUT - 4)
                act.wait_ge(s["mrg"], k + 1)
                act.activation(Hh[:, k, :], Of[:, k, :], ACT.Copy).then_inc(s["m_hi"], 1)

            def merge(j):
                for place in range(24):
                    if place % 2 == 0:
                        split_hi(act, j * 12 + SL_MERGE, place // 2 + LEAD)
                    if not again(j):
                        branches_high(place)
                    if is_last(j) and place >= 17:
                        for k in range(2 * (place - 17), 2 * (place - 17) + 2):
                            merged_high(k)
                    for v in range(2):
                        if place == 8 * v + 8:
                            act.wait_ge(s["used"], j * 12 + SL_MERGE + 4 * (v + 1))
                            if again(j):
                                act.wait_ge(s["mrg"], j)
                            act.activation(halves(sg[v][:, :]), acc(v), ACT.Exp, scale=-1.0).then_inc(s["m_e"], 1)
            merge(0)
            with act.Fori(1, KT - 1) as j:
                merge(j)
            merge(KT - 1)
            for k in (KT - 2, KT - 1):
                merged_high(k)
            act.wait_ge(s["used"], SL_OUT)

            def out_load(j, b):
                act.dma_start(xr[:, b, 0:NT, :], x_p[:, bass.ds(j * P, P)].rearrange("(t p) d -> p t d", p=P)).then_inc(x_tail[b], 16)
                act.dma_start(xr[0:NS, b, NT, :], x_s[:, bass.ds(j * P, P)]).then_inc(x_tail[b], 16)

            def out_unit(i, b, more):
                j = i * 2 + b
                for c in range(4):
                    if more or c + LEAD < 4:
                        split_hi(act, i * 8 + SL_OUT, 4 * b + c + LEAD)
                    if c == 0:
                        if again(i):
                            act.wait_ge(s["f_sb"], i * 2 + (b - 1))
                        out_load(j, b)
                    if c == 1 and (again(i) or b):
                        store(j - 1, 1 - b)

            def store(j, b):
                act.wait_ge(s["f_sb"], j + 1)
                act.dma_start(y_p[:, bass.ds(j * P, P)].rearrange("(t p) d -> p t d", p=P), yo[:, b, 0:NT, :]).then_inc(y_out[b], 16)
                act.dma_start(y_s[:, bass.ds(j * P, P)], yo[0:NS, b, NT, :]).then_inc(y_out[b], 16)
            for i in range(1):
                out_unit(0, 0, True)
                out_unit(0, 1, True)
            with act.Fori(1, KT // 2 - 1) as i:
                out_unit(i, 0, True)
                out_unit(i, 1, True)
            out_unit(KT // 2 - 1, 0, True)
            out_unit(KT // 2 - 1, 1, False)
            store(KT - 1, 1)
            act.wait_ge(s["y_out0"], 16 * KT)
            act.wait_ge(s["y_out1"], 16 * KT)
            act.wait_ge(s["cs_out"], 16 * 3)


        def both(view):
            return view[:, 0:NT, :], view[0:NS, NT, 0:NS]

        def both_ps():
            return tiles(G1), ps[0:NS, G2, 0:NS]

        def const_for(n):
            return con[:, n, :].unsqueeze(1).to_broadcast([P, NT, P]), con[0:NS, n, 0:NS]

        def keys_of(i):
            return (i + 1) * P if i < NT else PAST + NS

        def scores(i):
            return Pb[i % 2][0:rows_of(i), :, :].rearrange("p a n -> p (a n)")[:, 0:keys_of(i)]

        @block.vector
        def _(dve):
            link = Link(dve, s["dve_link"])
            stt = dve.scalar_tensor_tensor

            def conv(places, i):
                def first(h):
                    dve.wait_ge(s["cin_ready"], h * 3 + i + 1)
                    if i or again(h):
                        dve.wait_ge(s["act_ready"], h * 3 + i)
                    w = conv_cols[:, h + 8 * i, :]
                    link(dve.tensor_scalar(cacc[:, :], cin[:, 0:N + 3], w[:, 0:1], None, ALU.mult))
                    link(stt(cacc[:, :], cin[:, 1:N + 4], w[:, 1:2], cacc[:, :], ALU.mult, ALU.add))

                def second(h):
                    w = conv_cols[:, h + 8 * i, :]
                    link(stt(cacc[:, :], cin[:, 2:N + 5], w[:, 2:3], cacc[:, :], ALU.mult, ALU.add))
                    stt(cacc[:, :], cin[:, 3:N + 6], w[:, 3:4], cacc[:, :], ALU.mult, ALU.add).then_inc(s["conv_done"], 1)
                return [(places[0], first), (places[1], second)]

            def inverse_in_parts(places, ready, use):
                def part(n):
                    def go(h):
                        if n == 0:
                            ready(h)
                            link(dve.tensor_scalar(eT[:, :], eT[:, :], 1.0, None, ALU.add))
                        cols = slice(n * INV, min((n + 1) * INV, N + 3))
                        link(dve.reciprocal(eT[:, cols], eT[:, cols]))
                    return go
                return [(at, part(n)) for n, at in enumerate(places[:-1])] + [(places[-1], use)]

            def conv_e(i):
                def ready(h):
                    dve.wait_ge(s["exp_a"], h * 3 + i + 1)
                return ready

            def gate_e(sem):
                def ready(h):
                    dve.wait_ge(s[sem], h + 1)
                return ready

            def silu(i):
                def go(h):
                    if i == 0 and again(h):
                        dve.wait_ge(s["bnat_ps"], h * 3)
                    if i:
                        dve.wait_ge(s["nat_ps"], h * 3 + i)
                    dve.tensor_tensor(aT[:, 0:NP], cacc[:, 0:NP], eT[:, 0:NP], ALU.mult)
                    dve.tensor_tensor(aT[:, NP:N], cacc[:, NP + 3:N + 3], eT[:, NP + 3:N + 3], ALU.mult).then_inc(s["act_ready"], 1)
                return go

            def red_a(i):
                def go(h):
                    dve.wait_ge(s["sq_a"], h * 2 + i + 1)
                    if i == 0 and again(h):
                        dve.wait_ge(s["x_o"], h)
                    dve.tensor_reduce(st[:, SS_Q + i, :], sqb[:, :, :], AX.X, ALU.add).then_inc(s["ss_a"], 1)
                    if i:
                        dve.wait_ge(s["ss_a"], h * 2 + 2)
                        dve.tensor_scalar(st[:, X_Q:X_Q + 2, :], st[:, SS_Q:SS_Q + 2, :], EPS, None, ALU.add).then_inc(s["x_a"], 1)
                return go

            def scales(h):
                dve.wait_ge(s["y_a"], h + 1)
                if again(h):
                    dve.wait_ge(s["pool_a"], h * 5)
                rsqrt_newton(link, dve, st[:, Y_Q:Y_Q + 2, :], st[:, X_Q:X_Q + 2, :], st[:, T_Q:T_Q + 2, :])
                dve.tensor_scalar(st[:, SC_Q, :], st[:, Y_Q, :], float(P) ** -0.5, None, ALU.mult)
                link(dve.tensor_tensor(st[:, SC_KB, :], st[:, Y_K, :], beta[:, h, :], ALU.mult))
                dve.tensor_tensor(st[:, SC_QG, :], st[:, SC_Q, :], eG[:, h, :], ALU.mult)
                dve.tensor_tensor(st[:, SC_KBG, :], st[:, SC_KB, :], eG[:, h, :], ALU.mult)
                dve.tensor_tensor(st[:, SC_KG, :], st[:, Y_K, :], egl[:, h, :], ALU.mult).then_inc(s["scal_a"], 1)
                dve.wait_ge(s["scal_a"], h + 1)
                if again(h):
                    dve.wait_ge(s["pt_ps"], h * 5)
                dve.tensor_tensor(kn[:, :, :], k_nat[:, :, :], wide(st[:, Y_K, :]), ALU.mult).then_inc(s["knb_a"], 1)
                dve.tensor_tensor(kb[:, :, :], k_nat[:, :, :], wide(st[:, SC_KB, :]), ALU.mult).then_inc(s["knb_a"], 1)

            def decay(h):
                dve.wait_ge(s["grow_ps"], h + 1)
                dve.tensor_tensor(ET[:, 0:NT, :], tiles(G1), wide(Gc[:, h, 0:NT]), ALU.subtract)
                link(dve.tensor_tensor(ET[0:NS, NT, 0:NS], ps[0:NS, G2, 0:NS], Gc[0:NS, h, NT:NT + 1].to_broadcast([NS, NS]), ALU.subtract))
                for a, b in zip(both(ET), (s["diff"], None)):
                    ins = dve.tensor_scalar(a, a, 0.0, None, ALU.min)
                ins.then_inc(s["diff"], 1)



            def masked(ps_sem, em, factor, dst, sb_sem):
                def go(h):
                    dve.wait_ge(s[ps_sem], h + 1)
                    dve.wait_ge(s["em"], h * 2 + em)
                    for o, a, b in zip(both(dst), both_ps(), both(factor)):
                        ins = dve.tensor_tensor(o, a, b, ALU.mult)
                    ins.then_inc(s[sb_sem], 1)
                return go

            def first_level(src, dst, c):
                for o, a, b in zip(both(dst), both(src), const_for(c)):
                    ins = dve.tensor_tensor(o, a, b, ALU.mult)
                link(ins)
                for o, b in zip(both(dst), const_for(IDENT)):
                    ins = dve.tensor_tensor(o, o, b, ALU.add)
                return ins

            def first_level_s(h):
                dve.wait_ge(s["at"], h + 1)
                first_level(MT, Sm, PAIR_T)

            def first_level_t(h):
                dve.wait_ge(s["m"], h + 1)
                first_level(Mn, Tm, PAIR).then_inc(s["st0"], 1)

            def level_sub(n):
                def go(h):
                    dve.wait_ge(s["ly_ps"], h * 5 + n + 1)
                    for o, b in zip(both(Sm), both_ps()):
                        ins = dve.tensor_tensor(o, o, b, ALU.subtract)
                    ins.then_inc(s["ly"], 1)
                return go



            def chunk(n):
                return (0, NS, NT) if n == 0 else (CH * ((n - 1) % 2), CH, (n - 1) // 2)

            def v_new(n):
                def go(h):
                    r0, rows, t = chunk(n)
                    dve.wait_ge(s["sa_ps"], h * 9 + max(n, 1) + 1)
                    if n == 0:
                        dve.wait_ge(s["u_sb"], h + 1)
                        dve.tensor_tensor(Vs[:, :], U_[0:NS, NT, :], ps[0:NS, G1, P:2 * P], ALU.subtract).then_inc(s["vn"], 1)
                        return
                    dve.tensor_tensor(Vn[r0:r0 + rows, :], U_[r0:r0 + rows, t, :], ps[r0:r0 + rows, G1, 0:P], ALU.subtract).then_inc(s["vn"], 1)
                return go

            def state(n):
                def go(h):
                    r0, rows, t = chunk(n)
                    dve.wait_ge(s["sb_ps"], h * 9 + max(n, 1) + 1)
                    S, new = (St, ps[:, G2, 0:P]) if n else (Ss, ps[:, G2, P:2 * P])
                    stt(S[:, :], S[:, :], glb[:, r0 // CH, h, t:t + 1], new, ALU.mult, ALU.add).then_inc(s["ss_new"], 1)
                return go

            def red_o(h):
                dve.wait_ge(s["sq_o"], h + 1)
                link(dve.tensor_reduce(st[:, SS_Q, :], sqb[:, :, :], AX.X, ALU.add))
                dve.tensor_scalar(st[:, X_Q, :], st[:, SS_Q, :], 1.0 / P, EPS, ALU.mult, ALU.add).then_inc(s["x_o"], 1)

            def norm_o(h):
                dve.wait_ge(s["y_o"], h + 1)
                rsqrt_newton(link, dve, st[:, Y_Q, :], st[:, X_Q, :], st[:, T_Q, :])
                dve.tensor_tensor(o_nat[:, :, :], o_nat[:, :, :], wide(st[:, Y_Q, :]), ALU.mult).then_inc(s["on_o"], 1)

            def out_a(h):
                dve.wait_ge(s["o_ps"], h + 1)
                dve.wait_ge(s["sga"], h + 1)
                stt(Of[:, h, 0:NP], bank(G1), gnw_col, sga[:, 0:NP], ALU.mult, ALU.mult)
                stt(Of[:, h, NP:N], ps[:, G2, 0:NS], gnw_col, sga[:, NP:N], ALU.mult, ALU.mult).then_inc(s["oa"], 1)

            def gate(e_sem, z, sem):
                def go(h):
                    dve.tensor_tensor(z[:, :], z[:, :], eT[:, 0:N], ALU.mult).then_inc(s[sem], 1)
                return go

            def mask_bias(h):
                dve.wait_ge(s["bias_load"], h * 16 + 16)
                dve.memset(Bp[0:CH, 0:CH], MASKED).then_inc(s["bias"], 1)

            def red_b(i):
                def go(h):
                    dve.wait_ge(s["bsq"], h * 2 + i + 1)
                    if i == 0:
                        dve.tensor_reduce(st[:, SS_Q, :], sqb[:, :, :], AX.X, ALU.add).then_inc(s["bss"], 1)
                    else:
                        link(dve.tensor_reduce(st[:, SS_K, :], sqb[:, :, :], AX.X, ALU.add))
                        dve.tensor_scalar(st[:, X_Q:X_Q + 2, :], st[:, SS_Q:SS_Q + 2, :], 1.0 / P, EPS, ALU.mult, ALU.add).then_inc(s["x_b"], 1)
                return go

            def scale_b(h):
                dve.wait_ge(s["y_b"], h + 1)
                rsqrt_newton(link, dve, st[:, Y_Q:Y_Q + 2, :], st[:, X_Q:X_Q + 2, :], st[:, T_Q:T_Q + 2, :])
                link(dve.tensor_scalar(st[:, Y_Q, :], st[:, Y_Q, :], float(P) ** -0.5, None, ALU.mult))
                dve.tensor_tensor(bk[:, :, :], bk[:, :, :], wide(st[:, Y_K, :]), ALU.mult).then_inc(s["bk_y"], 1)
                dve.tensor_tensor(bq[:, :, :], bq[:, :, :], wide(st[:, Y_Q, :]), ALU.mult).then_inc(s["bqn"], 1)

            def soft(i):
                def go(h):
                    rows, n = rows_of(i), keys_of(i)
                    dve.wait_ge(s["qk"], h * 5 + i + 1)
                    if i == 0:
                        dve.wait_ge(s["bias"], h + 1)
                    if i < 2:
                        dve.wait_ge(s["ly_ps"], h * 5 + 5)
                    else:
                        dve.wait_ge(s["pt_ps"], h * 5 + i - 1)
                    p = scores(i)
                    width = {0: P, NT: P + NS}.get(i, 2 * P)
                    at = P if i == 0 else 0
                    near = Bp[0:rows, 2 * P - at - width:2 * P - at]
                    near = bass.AP(near.tensor, near.offset + width - 1, [list(near.ap[0]), [-1, width]])
                    if n > width:
                        dve.tensor_scalar(p[:, 0:n - width], ps[0:rows, A1, 0:n - width], Bp[0:rows, 2 * P - 1:2 * P], None, ALU.add)
                    dve.tensor_tensor(p[:, n - width:n], ps[0:rows, A1, n - width:n], near, ALU.add).then_inc(s["sadd"], 1)
                    dve.wait_ge(s["sadd"], h * 5 + i + 1)
                    dve.tensor_reduce(sm[0:rows, i % 2, 0:1], p, AX.X, ALU.max, negate=True).then_inc(s["smax"], 1)
                return go

            def prob(i):
                def go(h):
                    rows = rows_of(i)
                    dve.wait_ge(s["pexp"], h * 5 + i + 1)
                    link(dve.reciprocal(sm[0:rows, i % 2, 2:3], sm[0:rows, i % 2, 1:2]))
                    dve.tensor_scalar(scores(i), scores(i), sm[0:rows, i % 2, 2:3], None, ALU.mult).then_inc(s["pn"], 1)
                return go

            def out_b(i):
                def go(h):
                    rows = rows_of(i)
                    dve.wait_ge(s["pv"], h * 5 + i + 1)
                    if i == 0:
                        dve.wait_ge(s["sgb"], h + 1)
                    cols = slice(i * P, i * P + rows)
                    dve.tensor_tensor(Of[:, h + HEADS, cols], ps[:, A2, 0:rows], sgb[:, cols], ALU.mult).then_inc(s["ob"], 1)
                return go

            steps = [(71 + 4 * i + max(i - 2, 0), out_b(i)) for i in range(5)]
            steps += [(41 + 3 * n, level_sub(n)) for n in range(5)]
            steps += [(58 + 2 * max(n - 1, 0), v_new(n)) for n in range(9)] + [(59 + 2 * max(n - 1, 0), state(n)) for n in range(9)]
            steps += [(63 + 4 * i, soft(i)) for i in range(5)] + [(66 + 4 * i + max(i - 2, 0), prob(i)) for i in range(5)]
            steps += [(22, red_a(0)), (26, red_a(1)), (27, decay), (28, scales),
                     (35, masked("mt_ps", 1, ES, MT, "mt")), (36, masked("at_ps", 2, EU, AT, "at")), (37, first_level_s), (38, first_level_t),
                     (75, red_o), (77, norm_o), (80, out_a),
                     (49, red_b(0)), (53, red_b(1)), (55, scale_b), (50, mask_bias)]
            steps += conv((9, 10), 0) + conv((17, 17), 1) + conv((33, 33), 2)
            steps += inverse_in_parts((12, 12, 13, 14, 14, 15), conv_e(0), silu(0))
            steps += inverse_in_parts((19, 19, 20, 20, 20, 21), conv_e(1), silu(1))
            steps += inverse_in_parts((39, 39, 40, 42, 42, 43), conv_e(2), silu(2))
            steps += inverse_in_parts((46, 46, 47, 49, 49, 50), gate_e("ga_e"), gate("ga_e", sga, "sga"))
            steps += inverse_in_parts((65, 66, 67, 68, 69, 70), gate_e("gb_e"), gate("gb_e", sgb, "sgb"))
            steps.sort(key=lambda x: x[0])

            dve.memset(bar[:, :, :], 0.0)
            dve.memset(cw[:, :].bitcast(F32), 0.0)
            dve.memset(wbs[:, :].bitcast(F32), 0.0)
            for n in range(LEAD_START):
                start_lo(dve, n)
            dve.wait_ge(s["cT_e"], 1)
            link(dve.tensor_scalar(ce[:, :], ce[:, :], 1.0, None, ALU.add))
            link(dve.reciprocal(ce[:, :], ce[:, :]))
            dve.tensor_tensor(cvs[:, :, :], cv[:, :, :], ce[:, :].rearrange("p (g k) -> p k g", g=2), ALU.mult).then_inc(s["cT"], 1)

            dve.tensor_tensor(fold[:, :], eye[0:4, 0:2], eye[0:4, 2:4], ALU.add)
            dve.wait_ge(s["cw_hi"], 1)
            dve.tensor_tensor(cw4[:, :, 2:4], cvs[:, :, :], cw4[:, :, 0:2].bitcast(F32), ALU.subtract).then_inc(s["cw"], 1)

            def x_norm(t, k):
                rows = rows_of(t)
                if k == 2:
                    dve.wait_ge(s["x_ss"], t + 1)
                    dve.tensor_scalar(xs[0:rows, 1:2], xs[0:rows, 0:1], 1.0 / D, EPS, ALU.mult, ALU.add).then_inc(s["x_e"], 1)
                if k == 4:
                    dve.wait_ge(s["x_e"], 2 * t + 2)
                    y, x, z = xs[0:rows, 3:4], xs[0:rows, 1:2], xs[0:rows, 4:5]
                    link(dve.tensor_tensor(z, y, y, ALU.mult))
                    link(dve.tensor_tensor(z, z, x, ALU.mult))
                    link(dve.tensor_scalar(z, z, -0.5, 1.5, ALU.mult, ALU.add))
                    link(dve.tensor_tensor(y, y, z, ALU.mult))
                    dve.tensor_scalar(xn[t % 2][0:rows, :], xn[t % 2][0:rows, :], y, None, ALU.mult).then_inc(s["x_n"], 1)

            def mod_row(c):
                dve.wait_ge(s["used"], KT * (c + 1) if c < 8 else SL_GATE + KT * (c - 7))
                dve.tensor_copy(mrows[c // 8][:, :], ps[0:4 if c < 8 else 2, c % 2, :]).then_inc(s["ada_row"], 1)

            def mod_col(c, blk):
                dve.wait_ge(s["ada_cps"], c + 1)
                dve.tensor_tensor(modT[:, blk:blk + 4, :], ps[:, 2, 0:8].rearrange("p (b g) -> p b g", g=2),
                                  adab_cols[:, blk:blk + 4].unsqueeze(2).to_broadcast([P, 4, 2]), ALU.add).then_inc(s["ada_col"], 1)

            def h_scale(q):
                ks = slice(4 * q, 4 * q + 4)
                dve.wait_ge(s["xt"], 4 * (NT + 1))
                dve.wait_ge(s["ada_col"], 2 * q + 2)
                link(dve.tensor_scalar(hA[:, ks, :], modT[:, KT + 4 * q:KT + 4 * q + 4, :], 1.0, None, ALU.add))
                link(dve.tensor_tensor(hA[:, ks, :], hA[:, ks, :], norm_col[:, ks].unsqueeze(2).to_broadcast([P, 4, 2]), ALU.mult))

            def h_block(k):
                if k % 4 == 0:
                    h_scale(k // 4)
                dve.tensor_scalar(xT[:, k, 0:NP], xT[:, k, 0:NP], hA[:, k, 0:1], modT[:, k, 0:1], ALU.mult, ALU.add)
                dve.tensor_scalar(xT[:, k, NP:N], xT[:, k, NP:N], hA[:, k, 1:2], modT[:, k, 1:2], ALU.mult, ALU.add).then_inc(s["h_full"], 1)

            def mod_cols(c):
                mod_col(c, 4 * (c // 2) + (KT if c % 2 == 0 else 0))

            for c in range(8):
                for k in range(KT):
                    n = KT * c + k + LEAD_START
                    if n < SL_HEAD:
                        start_lo(dve, n)
                    elif n < SL_HEAD + LEAD:
                        split_lo(dve, SL_HEAD, n - SL_HEAD)
                    if c <= NT:
                        x_norm(c, k)
                    if k == 2 and c:
                        mod_row(c - 1)
                    if k == 7 and c:
                        mod_cols(c - 1)
                    if (c, k) in H_PLACES:
                        h_block(H_PLACES[c, k])
                    if c == 6 and k == 0:
                        dve.wait_ge(s["wba_hi"], 1)
                        dve.tensor_tensor(wbs2[:, :, 1, :], wba[:, :, :], wbs2[:, :, 0, :].bitcast(F32), ALU.subtract).then_inc(s["wba_lo"], 1)
            mod_row(7)
            mod_cols(7)
            for k in range(12, KT):
                h_block(k)

            a_in = bax[:, HEADS:2 * HEADS, :]

            def gate_in(h):
                dve.wait_ge(s["ba_sb"], 1)
                link(dve.tensor_tensor(bax[:, :, :], bar[:, :, 0:16].rearrange("p t n -> p n t"), bar[:, :, 16:32].rearrange("p t n -> p n t"), ALU.add))
                dve.wait_ge(s["row_load"], 48)
                link(dve.tensor_tensor(a_in, a_in, dtb[:, 0, :].unsqueeze(2).to_broadcast(gsz), ALU.add))
                link(dve.tensor_scalar(gt[1][:, :, :], a_in, -1.0, None, ALU.mult))
                dve.tensor_tensor(gt[1][:, :, :], gt[1][:, :, :], a_in, ALU.max).then_inc(s["g_e1"], 1)

            def gate_beta(h):
                dve.wait_ge(s["g_e2"], 1)
                link(dve.tensor_scalar(gt[0][:, :, :], gt[0][:, :, :], 1.0, None, ALU.add))
                dve.reciprocal(beta[:, :, :], gt[0][:, :, :])
                dve.tensor_scalar(gt[3][:, :, :], gt[2][:, :, :], 1.0, None, ALU.add).then_inc(s["g_e1"], 1)

            def gate_decay(h):
                dve.wait_ge(s["g_e1"], 2)
                stt(gt[5][:, :, :], gt[3][:, :, :], -1.0, gt[2][:, :, :], ALU.add, ALU.subtract)
                link(dve.reciprocal(gt[0][:, :, :], gt[3][:, :, :]))
                link(dve.tensor_tensor(gt[5][:, :, :], gt[5][:, :, :], gt[0][:, :, :], ALU.mult))
                dve.wait_ge(s["g_e3"], 1)
                link(dve.tensor_tensor(gt[4][:, :, :], gt[4][:, :, :], gt[5][:, :, :], ALU.subtract))
                link(stt(gt[4][:, :, :], a_in, 0.0, gt[4][:, :, :], ALU.max, ALU.add))
                link(stt(gg[:, :, :], gt[4][:, :, :], -1.0, dtb[:, 1, :].unsqueeze(2).to_broadcast(gsz), ALU.mult, ALU.mult))
                dve.memset(gg[NS:2 * NS, :, NT], 0.0)
                dve.memset(gg[2 * NS:P, :, NT], 0.0).then_inc(s["g_g"], 1)

            def gate_rest(h):
                dve.wait_ge(s["cum_sb"], 1)
                dve.tensor_tensor(gt[1][:, :, :], gt[0][:, :, :], Gc[:, :, :], ALU.subtract).then_inc(s["cum_d"], 1)

            def gates_there(h):
                dve.wait_ge(s["gates"], 1)

            def body(h, last=False):
                for place in range(GRID):
                    if place % 2 == 0 and not (last and place // 2 + LEAD >= 32):
                        split_lo(dve, h * 32 + SL_HEAD, place // 2 + LEAD)
                    if not again(h):
                        run_head([(10, gate_in), (11, gate_beta), (12, gate_decay), (15, gate_rest), (17, gates_there)], h, place)
                    run_head(steps, h, place)
            body(0)
            with dve.Fori(1, HEADS - 1) as h:
                link.loop(h, 1, DVE_LINKS)
                body(h)
            link.end(HEADS - 2)
            body(HEADS - 1, True)

            for place in range(32):
                run_tail(steps, place)
                if place % 8 == 7:
                    mod_row(8 + place // 8)
                if place % 8 == 1 and place > 8:
                    mod_col(8 + place // 8 - 1, 2 * KT + 4 * (place // 8 - 1))
            mod_col(11, 2 * KT + 12)
            for c in range(LEAD):
                split_lo(dve, SPLIT_MERGE, c)

            def merged_low(k):
                dve.wait_ge(s["m_hi"], k + 1)
                dve.tensor_tensor(Hl[:, k, :], Of[:, k, :], Hh[:, k, :].bitcast(F32), ALU.subtract).then_inc(s["m_lo"], 1)

            def merge(j):
                for place in range(24):
                    if place % 2 == 0:
                        split_lo(dve, j * 12 + SPLIT_MERGE, place // 2 + LEAD)
                    if not again(j) and 3 <= place < 3 + KT // 2:
                        for k in (2 * (place - 3), 2 * (place - 3) + 1):
                            dve.wait_ge(s["o_hi"], k + 1)
                            dve.tensor_tensor(Ol[:, k, :], Of[:, k, :], Oh[:, k, :].bitcast(F32), ALU.subtract).then_inc(s["o_lo"], 1)
                    if is_last(j) and place >= 18:
                        for k in range(2 * (place - 18), 2 * (place - 18) + 2):
                            merged_low(k)
                    for v in range(2):
                        if place == 8 * v + 9:
                            dve.wait_ge(s["m_e"], j * 2 + v + 1)
                            link(dve.tensor_scalar(sg[v][:, :], sg[v][:, :], 1.0, None, ALU.add))
                            dve.reciprocal(sg[v][:, :], sg[v][:, :]).then_inc(s["m_sig"], 1)
                    if place == 20:
                        dve.wait_ge(s["used"], j * 12 + SL_MERGE + 10)
                        dve.wait_ge(s["m_sig"], j * 2 + 2)
                        dve.tensor_tensor(halves(tmp[:, :]), acc(0), halves(sg[0][:, :]), ALU.mult).then_inc(s["mrg_a"], 1)
                dve.wait_ge(s["used"], j * 12 + SL_MERGE + 12)
                link(dve.tensor_tensor(halves(sg[1][:, :]), acc(1), halves(sg[1][:, :]), ALU.mult))
                dve.tensor_tensor(Of[:, j, :], tmp[:, :], sg[1][:, :], ALU.add).then_inc(s["mrg"], 1)
            merge(0)
            with dve.Fori(1, KT - 1) as j:
                link.loop(j, 1, 3)
                merge(j)
            link.end(KT - 2)
            merge(KT - 1)
            for k in range(12, KT):
                merged_low(k)

            def out_unit(i, b, more):
                j = i * 2 + b
                for c in range(4):
                    if more or c + LEAD < 4:
                        split_lo(dve, i * 8 + SPLIT_OUT, 4 * b + c + LEAD)
                    if c == 1 and b:
                        residual(i, 0)
                    if c == 1 and not b and again(i):
                        residual(i - 1, 1)
                dve.wait_ge(s["used"], j * 4 + SL_OUT + 4)
                if again(i):
                    dve.wait_ge(s["f_ps"], j - 1)
                gcol = modT[:, j + 2 * KT, :]
                dve.tensor_scalar(fo[:, b, 0:HALF], ps[:, 2 * b, 0:HALF], gcol[:, 0:1], None, ALU.mult)
                dve.tensor_scalar(fo[:, b, HALF:NP], ps[:, 2 * b + 1, 0:NP - HALF], gcol[:, 0:1], None, ALU.mult)
                dve.tensor_scalar(fo[:, b, NP:N], ps[:, 2 * b + 1, NP - HALF:HALF], gcol[:, 1:2], None, ALU.mult).then_inc(s["f_g"], 1)

            def residual(i, b, first=False):
                dve.wait_ge(s["f_ps"], i * 2 + b + 1)
                dve.wait_ge(x_tail[b], i * 32 + 32)
                if again(i) and not first:
                    dve.wait_ge(y_out[b], i * 32)
                dve.tensor_tensor(yo[:, b, 0:NT, :], tiles(G1), xr[:, b, 0:NT, :], ALU.add)
                dve.tensor_tensor(yo[0:NS, b, NT, :], ps[0:NS, G2, 0:P], xr[0:NS, b, NT, :], ALU.add).then_inc(s["f_sb"], 1)
            out_unit(0, 0, True)
            out_unit(0, 1, True)
            with dve.Fori(1, KT // 2 - 1) as i:
                out_unit(i, 0, True)
                out_unit(i, 1, True)
            out_unit(KT // 2 - 1, 0, True)
            out_unit(KT // 2 - 1, 1, False)
            residual(KT // 2 - 1, 1)

        @block.gpsimd
        def _(pool):
            mul = ALU.mult

            def tails(i):
                def go(h):
                    pool.wait_ge(s["cin_ready"], h * 3 + i + 1)
                    pool.tensor_copy(cs[:, 0:3, h + 8 * i], cin[:, NP:NP + 3])
                    pool.tensor_copy(cs[:, 3:6, h + 8 * i], cin[:, N + 3:N + 6]).then_inc(s["tails"], 1)
                return go

            def square_a(i):
                def go(h):
                    src = (q_nat, k_nat)[i]
                    pool.wait_ge(s["nat_a"], h * 3 + i + 1)
                    if i:
                        pool.wait_ge(s["ss_a"], h * 2 + 1)
                    elif again(h):
                        pool.wait_ge(s["x_o"], h)
                    pool.tensor_tensor(sqb[:, :, :], src[:, :, :], src[:, :, :], mul).then_inc(s["sq_a"], 1)
                return go

            def g_wide(h):
                if again(h):
                    pool.wait_ge(s["pt_ps"], h * 5)
                pool.tensor_copy(gbc[:, :, :], wide(gg[:, h, :])).then_inc(s["gbc"], 1)

            def scaled(h):
                pool.wait_ge(s["scal_a"], h + 1)
                if again(h):
                    pool.wait_ge(s["sb_ps"], h * 9)
                for dst, src, c in ((qn, q_nat, SC_Q), (qg, q_nat, SC_QG), (kbg, k_nat, SC_KBG), (kg, k_nat, SC_KG)):
                    pool.tensor_tensor(dst[:, :, :], src[:, :, :], wide(st[:, c, :]), mul).then_inc(s["pool_a"], 1)

            def scaled_v(h):
                pool.wait_ge(s["nat_a"], h * 3 + 3)
                pool.tensor_tensor(vb[:, :, :], v_nat[:, :, :], wide(beta[:, h, :]), mul).then_inc(s["pool_a"], 1)

            def zero_state(h):
                if again(h):
                    pool.wait_ge(s["s_out"], h * 32)
                pool.tensor_tensor(St[:, :], eye[:, :], eye[:, :], ALU.subtract).then_inc(s["s_zero"], 1)

            def mask_decay(h):
                pool.wait_ge(s["et"], h + 1)
                for dst, c in ((ES, STRICT), (EU, UPPER)):
                    for o, a, b in zip(both(dst), both(ET), const_for(c)):
                        ins = pool.tensor_tensor(o, a, b, mul)
                    ins.then_inc(s["em"], 1)

            def level_mask(n):
                def go(h):
                    if n == 0:
                        pool.wait_ge(s["m"], h + 1)
                    if n >= 2:
                        pool.wait_ge(s["lx_ps"], h * 5 + n - 1)
                    for o, a, b in zip(both((B0, B1)[n % 2]), both(Mn), const_for(LEVEL2 + n)):
                        ins = pool.tensor_tensor(o, a, b, mul)
                    ins.then_inc(s["bm"], 1)
                return go

            def square_o(h):
                pool.wait_ge(s["so"], h * 9 + 9)
                pool.wait_ge(s["x_b"], h + 1)
                pool.tensor_tensor(sqb[:, :, :], o_nat[:, :, :], o_nat[:, :, :], mul).then_inc(s["sq_o"], 1)

            def square_b(i):
                def go(h):
                    src = (bq, bk)[i]
                    pool.wait_ge(s["bnat"], h * 3 + i + 1)
                    if i:
                        pool.wait_ge(s["bss"], h + 1)
                    pool.tensor_tensor(sqb[:, :, :], src[:, :, :], src[:, :, :], mul).then_inc(s["bsq"], 1)
                return go

            def k_weight(h):
                pool.wait_ge(s["bk_y"], h + 1)
                if not again(h):
                    pool.wait_ge(s["row_load"], 48)
                pool.tensor_tensor(bk[:, :, :], bk[:, :, :], kwb[:, :].unsqueeze(1).to_broadcast([P, NT + 1, P]), mul).then_inc(s["bkw"], 1)

            steps = [(9, tails(0)), (17, tails(1)), (25, tails(2)), (20, square_a(0)), (25, square_a(1)), (23, g_wide),
                     (28, scaled), (45, scaled_v), (31, zero_state), (31, mask_decay), (74, square_o),
                     (47, square_b(0)), (52, square_b(1)), (56, k_weight)]
            steps += [(38 + 3 * n, level_mask(n)) for n in range(5)]
            steps.sort(key=lambda x: x[0])

            pool.dma_start(vrow[0:96, 0, :], io["conv_w"].rearrange("o i (b c) -> (o i b) c", c=P)).then_inc(s["v_load"], 16)
            pool.dma_start(vrow[96:112, 0, :], io["norm_w"].rearrange("o (b c) -> (o b) c", c=P)).then_inc(s["v_load"], 16)
            pool.dma_start(vrow[112:113, 0, :], io["gdn_norm_w"]).then_inc(s["v_load"], 16)
            pool.dma_start(vrow[113:114, 0, :], io["q_norm_w"]).then_inc(s["v_load"], 16)
            pool.dma_start(vrow[0:72, 1, :], io["state_conv"].rearrange("o b i (c d) -> (o b i c) d", d=P)).then_inc(s["v_load"], 16)
            pool.dma_start(vrow[72:120, 1, :], io["ada_b"].rearrange("o (b c) -> (o b) c", c=P)).then_inc(s["v_load"], 16)
            pool.dma_start(con[:, :, :], io["con"]).then_inc(s["v_load"], 16)
            pool.dma_start(wba[:, :, :], w_in[:, COL_BA:COL_BA + 16].rearrange("(k p) n -> p k n", p=P)).then_inc(s["wba_load"], 16)
            pool.dma_start(kwb[:, :], bass.AP(io["k_norm_w"].tensor, io["k_norm_w"].offset, [[0, P], [1, P]])).then_inc(s["row_load"], 16)
            for n, name in enumerate(("gdn_dt_bias", "gdn_a_log")):
                row = io[name]
                pool.dma_start(dtb[:, n, :], bass.AP(row.tensor, row.offset, [[0, P], [1, HEADS]])).then_inc(s["row_load"], 16)
            for k in range(KT):
                pool.wait_ge(s["h_hi"], k + 1)
                pool.tensor_tensor(Hl[:, k, :], xT[:, k, :], Hh[:, k, :].bitcast(F32), ALU.subtract).then_inc(s["h_lo"], 1)
            pool.wait_ge(s["h_lo"], KT)
            for b in (q_nat, k_nat, v_nat, sqb, Mn, B0, B1, MT, AT, Sm, Tm, Xs, vb, kbg, kg):
                pool.memset(b[:, NT, :], 0.0)
            pool.memset(cin[:, 0:3], 0.0).then_inc(s["zeroed"], 1)
            pool.wait_ge(s["zeroed"], 1)

            def gates_there(h):
                pool.wait_ge(s["gates"], 1)
                pool.memset(bv[:, NT, :], 0.0).then_inc(s["zeroed"], 1)
                pool.wait_ge(s["zeroed"], 2)

            def body(h):
                for place in range(GRID):
                    if not again(h):
                        run_head([(16, gates_there)], h, place)
                    run_head(steps, h, place)
            body(0)
            with pool.Fori(1, HEADS) as h:
                body(h)
            for place in range(32):
                run_tail(steps, place)

        @block.tensor
        def _(pe):
            mm = pe.matmul

            def turn(out, in_, rows=P):
                return pe.transpose(out, in_, eye[0:rows, 0:rows])

            def to_nat(src, b):
                for t in range(NT):
                    turn(ps[:, b, t * P:(t + 1) * P], src[:, t * P:(t + 1) * P])
                return turn(ps[0:NS, b + 1, 0:P], src[:, NP:N])

            def to_T(src, b):
                for t in range(NT):
                    turn(ps[:, b, t * P:(t + 1) * P], src[:, t, :])
                return turn(ps[:, b + 1, 0:NS], src[0:NS, NT, :], NS)

            def nat_a(i):
                def go(h):
                    pe.wait_ge(s["act_ready"], h * 3 + i + 1)
                    if i == 0:
                        pe.wait_ge(s["oa"] if again(h) else s["cum_sb"], h if again(h) else 1)
                    if i == 1:
                        pe.wait_ge(s["nat_a"], h * 3 + 1)
                    if i == 2 and again(h):
                        pe.wait_ge(s["ob"], h * 5)
                    to_nat(aT, G1 if i < 2 else A1).then_inc(s["nat_ps"], 1)
                return go

            def grow(h):
                pe.wait_ge(s["gbc"], h + 1)
                pe.wait_ge(s["nat_a"], h * 3 + 2)
                for t in range(NT):
                    mm(ps[:, G1, t * P:(t + 1) * P], gbc[:, t, :], con[:, UPPER, :], start=True, stop=True)
                mm(ps[0:NS, G2, 0:NS], gbc[0:NS, NT, 0:NS], con[0:NS, UPPER, 0:NS], start=True, stop=True).then_inc(s["grow_ps"], 1)

            def tr_a(n):
                def go(h):
                    if n == 0:
                        pe.wait_ge(s["knb_a"], h * 2 + 1)
                        pe.wait_ge(s["diff"], h + 1)
                    if n == 1:
                        pe.wait_ge(s["knb_a"], h * 2 + 2)
                        pe.wait_ge(s["tra_act"], h * 3 + 1)
                    if n == 2:
                        pe.wait_ge(s["pool_a"], h * 5 + 1)
                        pe.wait_ge(s["kbt"], h + 1)
                    if n == 3:
                        pe.wait_ge(s["pool_a"], h * 5 + 2)
                        pe.wait_ge(s["tra_act"], h * 3 + 2)
                    to_T((kn, kb, qn, qg)[n], G1).then_inc(s["tr_a"], 1)
                return go

            def outer(right, wait_sem, per, count, sem):
                def go(h):
                    pe.wait_ge(s[wait_sem], h * per + count)
                    for t in range(NT):
                        c = slice(t * P, (t + 1) * P)
                        mm(ps[:, G1, c], knT[:, c], right[:, c], start=True, stop=True)
                    mm(ps[0:NS, G2, 0:NS], knT[:, NP:N], right[:, NP:N], start=True, stop=True).then_inc(s[sem], 1)
                return go

            def turn_square(src):
                for t in range(NT):
                    turn(ps[:, G1, t * P:(t + 1) * P], src[:, t, :])
                return turn(ps[0:NS, G2, 0:NS], src[0:NS, NT, 0:NS], NS)

            def m_turn(h):
                pe.wait_ge(s["at"], h + 1)
                turn_square(MT).then_inc(s["m_ps"], 1)

            def square_product(left, right):
                for t in range(NT):
                    mm(ps[:, G1, t * P:(t + 1) * P], left[:, t, :], right[:, t, :], start=True, stop=True)
                return mm(ps[0:NS, G2, 0:NS], left[0:NS, NT, 0:NS], right[0:NS, NT, 0:NS], start=True, stop=True)

            def level_x(n):
                def go(h):
                    if n == 0:
                        pe.wait_ge(s["st0"], h + 1)
                    else:
                        pe.wait_ge(s["lt"], h * 4 + n)
                    pe.wait_ge(s["bm"], h * 5 + n + 1)
                    square_product((B0, B1)[n % 2], Sm).then_inc(s["lx_ps"], 1)
                return go

            def level_y(n):
                def go(h):
                    pe.wait_ge(s["lx"], h * 5 + n + 1)
                    square_product(Tm, Xs).then_inc(s["ly_ps"], 1)
                return go

            def level_t(n):
                def go(h):
                    pe.wait_ge(s["ly"], h * 5 + n + 1)
                    turn_square(Sm).then_inc(s["lt_ps"], 1)
                return go

            def w_rows(h):
                pe.wait_ge(s["ly"], h * 5 + 5)
                pe.wait_ge(s["pool_a"], h * 5 + 5)
                for t in range(NT):
                    mm(ps[:, G1, t * P:(t + 1) * P], kbg[:, t, :], Sm[:, t, :], start=True, stop=True)
                mm(ps[:, G2, 0:NS], kbg[0:NS, NT, :], Sm[0:NS, NT, 0:NS], start=True, stop=True).then_inc(s["w_ps"], 1)

            def u_rows(h):
                pe.wait_ge(s["w_sb"], h + 1)
                for t in range(NT):
                    mm(ps[:, G1, t * P:(t + 1) * P], Sm[:, t, :], vb[:, t, :], start=True, stop=True)
                mm(ps[0:NS, G2, 0:P], Sm[0:NS, NT, 0:NS], vb[0:NS, NT, :], start=True, stop=True).then_inc(s["u_ps"], 1)

            def chunk_state(n):
                def go(h):
                    if n == 1:
                        pe.wait_ge(s["u_sb"], h + 1)
                        pe.wait_ge(s["s_zero"], h + 1)
                    else:
                        pe.wait_ge(s["so"], h * 9 + n)
                        pe.wait_ge(s["ss_new"], h * 9 + n)
                    mm(ps[:, G1, 0:P], qgw[:, (n - 1) * P:n * P], St[:, :], start=True, stop=True).then_inc(s["sa_ps"], 1)
                    if n == 1:
                        pe.wait_ge(s["s_load"], h * 16 + 16)
                        mm(ps[0:2 * NS, G1, P:2 * P], qgw[:, NCH * P:NCH * P + 2 * NS], Ss[:, :], start=True, stop=True).then_inc(s["sa_ps"], 1)
                return go

            def chunk_new(n):
                def go(h):
                    pe.wait_ge(s["vn"], h * 9 + n + 1)
                    if n == 1:
                        mm(ps[:, G2, P:2 * P], kg[0:NS, NT, :], Vs[:, :], start=True, stop=True)
                        mm(ps[NS:2 * NS, G1, P:2 * P], AT[0:NS, NT, 0:NS], Vs[:, :], start=False, stop=True, skip_group_check=True).then_inc(s["sb_ps"], 1)
                    r0 = CH * ((n - 1) % 2)
                    o0, rows, t = CH - r0, CH, (n - 1) // 2
                    k = slice(r0, r0 + rows)
                    mm(ps[:, G2, 0:P], kg[k, t, :], Vn[k, :], start=True, stop=True)
                    mm(ps[o0:o0 + rows, G1, 0:P], AT[k, t, k], Vn[k, :], start=False, stop=True, skip_group_check=True).then_inc(s["sb_ps"], 1)
                return go

            def o_turn(h):
                pe.wait_ge(s["on_o"], h + 1)
                to_T(o_nat, G1).then_inc(s["o_ps"], 1)

            def nat_b(i):
                def go(h):
                    pe.wait_ge(s["bz"], h * 3 + i + 1)
                    if i == 0:
                        pe.wait_ge(s["nat_a"], h * 3 + 3)
                    if i == 1:
                        pe.wait_ge(s["ct"], h + 1)
                    if i == 2:
                        pe.wait_ge(s["btr"], h * 2 + 1)
                    to_nat(aT, A1).then_inc(s["bnat_ps"], 1)
                return go

            def cache_turn(h):
                pe.wait_ge(s["cache_load"], h * 32 + 32)
                pe.wait_ge(s["bnat"], h * 3 + 1)
                for a in range(2):
                    ins = turn(ps[:, A1, a * P:(a + 1) * P], kc[:, a, :])
                ins.then_inc(s["ct_ps"], 1)

            def tr_b(n):
                def go(h):
                    if n == 0:
                        pe.wait_ge(s["bkw"], h + 1)
                        pe.wait_ge(s["bnat"], h * 3 + 2)
                    else:
                        pe.wait_ge(s["bqn"], h + 1)
                        pe.wait_ge(s["bnat"], h * 3 + 3)
                    to_T((bk, bq)[n], A1).then_inc(s["btr_ps"], 1)
                return go

            def score(i):
                def go(h):
                    if i == 0:
                        pe.wait_ge(s["btr"], h * 2 + 2)
                    else:
                        pe.wait_ge(s["sadd"], h * 5 + i)
                    if i < NT:
                        ins = mm(ps[:, A1, 0:(i + 1) * P], qT[:, i * P:(i + 1) * P], kT[:, 0:(i + 1) * P], start=True, stop=True)
                    else:
                        mm(ps[0:NS, A1, 0:PAST], qT[:, NP:N], kcT[:, :], start=True, stop=True)
                        ins = mm(ps[0:NS, A1, PAST:PAST + NS], qT[:, NP:N], kT[:, NP:N], start=True, stop=True)
                    ins.then_inc(s["qk"], 1)
                return go

            def prob_turn(i):
                def go(h):
                    pe.wait_ge(s["pn"], h * 5 + i + 1)
                    if i:
                        pe.wait_ge(s["ob"], h * 5 + i)
                    p = scores(i)
                    if i < NT:
                        for t in range(i + 1):
                            ins = turn(ps[:, A2, t * P:(t + 1) * P], p[:, t * P:(t + 1) * P])
                    else:
                        mm(ps[:, A2, 0:NS], p[:, 0:P], eye[0:NS, 0:NS], start=True, stop=True)
                        turn(ps[:, A2, NS:2 * NS], p[:, P:2 * P], NS)
                        ins = turn(ps[0:NS, A2, 2 * NS:3 * NS], p[:, PAST:PAST + NS], NS)
                    ins.then_inc(s["pt_ps"], 1)
                return go

            def values(i):
                def go(h):
                    pe.wait_ge(s["pt"], h * 5 + i + 1)
                    if i < NT:
                        for t in range(i + 1):
                            ins = mm(ps[:, A2, 0:P], bv[:, t, :], PT[:, t * P:(t + 1) * P], start=t == 0, stop=t == i)
                    else:
                        for t in range(2):
                            mm(ps[:, A2, 0:NS], vc[:, t, :], PT[:, t * NS:(t + 1) * NS], start=t == 0, stop=False)
                        ins = mm(ps[:, A2, 0:NS], bv[0:NS, NT, :], PT[0:NS, 2 * NS:3 * NS], start=False, stop=True)
                    ins.then_inc(s["pv"], 1)
                return go

            steps = [(18, nat_a(0)), (24, nat_a(1)), (26, grow), (31, tr_a(0)), (44, nat_a(2)), (32, tr_a(1)), (33, tr_a(2)),
                     (34, tr_a(3)), (35, outer(kbT, "tra_act", 3, 3, "mt_ps")), (36, outer(qnT, "mt", 1, 1, "at_ps")), (37, m_turn),
                     (55, w_rows), (56, u_rows), (79, o_turn),
                     (46, nat_b(0)), (49, cache_turn), (51, nat_b(1)), (58, tr_b(0)), (59, nat_b(2)), (60, tr_b(1))]
            for n in range(5):
                steps += [(40 + 3 * n, level_x(n)), (41 + 3 * n, level_y(n))]
                if n < 4:
                    steps.append((42 + 3 * n, level_t(n)))
            steps += [(58 + 2 * n, chunk_state(n + 1)) for n in range(8)] + [(59 + 2 * n, chunk_new(n + 1)) for n in range(8)]
            steps += [(62 + 4 * i, score(i)) for i in range(5)] + [(68 + 4 * i + max(i - 2, 0), prob_turn(i)) for i in range(5)]
            steps += [(70 + 4 * i + max(i - 2, 0), values(i)) for i in range(5)]
            steps.sort(key=lambda x: x[0])

            def products(base, c, half, Xh, Xl, k0, pair, start, stop):
                r = c % RING
                if half == 0:
                    pe.wait_ge(s["lo"], base + (c + 1))
                for n in range(2):
                    w = slice((2 * half + n) * P, (2 * half + n + 1) * P)
                    k = k0 + n
                    passes = [(whi, Xh), (whi, Xl), (wlo, Xh)]
                    for m, (weights, X) in enumerate(passes):
                        for a in range(2):
                            ins = mm(ps[:, 2 * pair + a, 0:HALF], weights[:, r, w], X[:, k, a * HALF:(a + 1) * HALF],
                                     start=start and n == 0 and m == 0, stop=stop and n == 1 and m == 2)
                if half == 1:
                    ins.then_inc(s["used"], 1)

            pe.wait_ge(s["c_load"], 16 * 3)
            turn(ps[:, G2, 0:2 * KT], crow[:, :], 2 * KT).then_inc(s["cT_ps"], 1)

            def ada_slot(n, c, k):
                if n == 0:
                    pe.wait_ge(s["cw"], 1)
                if k == 0 and c >= 2:
                    pe.wait_ge(s["ada_row"], c - 1)
                pe.wait_ge(s["lo"], n + 1)
                for m, weights in enumerate(start_parts(n)):
                    ins = mm(ps[:, c % 2, :], cw[:, 4 * k:4 * k + P], weights, start=k == 0 and m == 0, stop=k == KT - 1 and m == 1)
                ins.then_inc(s["used"], 1)

            def gate_slot(n, c, k):
                if k == 0:
                    pe.wait_ge(s["ada_row"], c - 1)
                r = n % RING
                pe.wait_ge(landed[r], 16 * ((n - SL_HEAD) // RING + 1) + LANDED_START)
                mm(ps[0:2, c % 2, :], cvs[:, k, :], raw[:, r, :], start=k == 0, stop=k == KT - 1).then_inc(s["used"], 1)

            def mod_turn(c):
                pe.wait_ge(s["ada_row"], c + 1)
                if c:
                    pe.wait_ge(s["ada_col"], c)
                for b in range(4):
                    ins = mm(ps[:, 2, 2 * b:2 * b + 2], mrows[c // 8][:, b * P:(b + 1) * P], fold[:, :] if c < 8 else eye[0:2, 0:2],
                             start=True, stop=True)
                ins.then_inc(s["ada_cps"], 1)

            def x_turn(t, q):
                rows = rows_of(t)
                pe.wait_ge(s["x_n"], t + 1)
                if 4 * t + q >= 2:
                    pe.wait_ge(s["xt"], 4 * t + q - 1)
                for b in range(4):
                    k = 4 * q + b
                    ins = turn(ps[:, G1 + q % 2, b * P:b * P + rows], xn[t % 2][0:rows, k * P:(k + 1) * P], rows)
                ins.then_inc(s["xt_ps"], 1)

            for c in range(8):
                for k in range(KT):
                    ada_slot(KT * c + k, c, k)
                    if k == 6 and c:
                        mod_turn(c - 1)
                    if c <= NT and k in (8, 10, 12, 14):
                        x_turn(c, (k - 8) // 2)
                    if (c, k) == (0, 14):
                        pe.wait_ge(s["v_load"], 16 * 7)
                        turn(ps[:, A1, 0:114], vrow[0:114, 0, :], 114)
                        turn(ps[:, A1, P:P + 120], vrow[0:120, 1, :], 120).then_inc(s["vec_ps"], 1)
            mod_turn(7)

            def beta_rows(h):
                pe.wait_ge(s["wba_lo"], 1)
                pe.wait_ge(s["xt"], 4 * (NT + 1))
                for k in range(KT):
                    for m, X in enumerate((Hh, Hl)):
                        for a in range(2):
                            ins = mm(ps[:, G1 + a, 0:HALF], wbs[:, 32 * k:32 * k + P], X[:, k, a * HALF:(a + 1) * HALF],
                                     start=k == 0 and m == 0, stop=k == KT - 1 and m == 1)
                ins.then_inc(s["ba_ps"], 1)

            def beta_turn(h):
                pe.wait_ge(s["baT"], 1)
                for t in range(NT + 1):
                    rows = rows_of(t)
                    ins = turn(ps[0:rows, A1, 32 * t:32 * t + 32], baT[:, t * P:t * P + rows], 32)
                ins.then_inc(s["ba_turn"], 1)

            def cumulate(h):
                pe.wait_ge(s["g_g"], 1)
                g = gg[:, :, :].rearrange("p h t -> p (h t)")
                for n, c in enumerate((UPPER, BLOCK, ROWS_A, ROWS_B)):
                    ins = mm(ps[:, G2, n * NG:(n + 1) * NG], con[:, c, :], g, start=True, stop=True)
                ins.then_inc(s["cum_ps"], 1)

            def pair_free(u, h):
                if u == 0 and again(h):
                    pe.wait_ge(s["bz"], h * 3)
                if u == 0 and not again(h):
                    pe.wait_ge(s["ada_row"], 8)
                if u == 1:
                    if again(h):
                        pe.wait_ge(s["gb_z"], h)
                    else:
                        pe.wait_ge(s["ada_col"], 8)
                if 2 <= u <= 4:
                    pe.wait_ge(s["cin_ready"], h * 3 + u - 1)
                if u == 5:
                    pe.wait_ge(s["ga_z"], h + 1)
                if u >= 6:
                    pe.wait_ge(s["bz"], h * 3 + u - 5)

            def body(h):
                for place in range(GRID):
                    u, part = divmod(place, 8)
                    if part == 0 and u > 0:
                        pair_free(u, h)
                    if place == 0:
                        pair_free(0, h)
                    if not again(h) and u == 0:
                        pe.wait_ge(s["h_lo"], 2 * part + 2)
                    products(h * 32 + SL_HEAD, place // 2, place % 2, Hh, Hl, 2 * part, u % 2, part == 0, part == 7)
                    if not again(h):
                        run_head([(8, beta_rows), (9, beta_turn), (13, cumulate)], h, place)
                    run_head(steps, h, place)
            body(0)
            with pe.Fori(1, HEADS) as h:
                body(h)

            for g in range(4 * KT):
                c, k = 8 + g // KT, g % KT
                if g == 0:
                    pe.wait_ge(s["bz"], 3 * HEADS)
                gate_slot(SL_GATE + g, c, k)
                if k == 3 and c > 8:
                    pe.wait_ge(s["gb_z"], HEADS)
                    mod_turn(c - 1)
                if g % 2 == 0:
                    run_tail(steps, g // 2)
            mod_turn(11)
            pe.wait_ge(s["tails"], 3 * HEADS)
            csr = cs[:, :, :].rearrange("p i b -> p (i b)")
            pe.wait_ge(s["sadd"], 5 * HEADS)
            turn(ps[:, A1, 0:P], csr[:, 0:P])
            turn(ps[0:16, A1, P:2 * P], csr[:, P:P + 16]).then_inc(s["cs_ps"], 1)

            def merge(j):
                for u, (c0, count, Xh, Xl, k0) in enumerate(((0, 4, Hh, Hl, 0), (4, 4, Hh, Hl, 0), (8, 2, Oh, Ol, 0), (10, 2, Oh, Ol, 8))):
                    if u < 2:
                        if again(j):
                            pe.wait_ge(s["mrg_a" if u == 0 else "mrg"], j)
                        else:
                            pe.wait_ge(s["ada_row"] if u == 0 else s["ada_col"], 12)
                    else:
                        pe.wait_ge(s["m_e"], j * 2 + u - 1)
                    for n in range(2 * count):
                        if u >= 2 and not again(j):
                            pe.wait_ge(s["o_lo"], k0 + 2 * n + 2)
                        products(j * 12 + SPLIT_MERGE, c0 + n // 2, n % 2, Xh, Xl, k0 + 2 * n, u % 2, n == 0, n == 2 * count - 1)
            merge(0)
            with pe.Fori(1, KT) as j:
                merge(j)

            def out_turn(j, b):
                pe.wait_ge(s["f_g"], j + 1)
                if again(j):
                    pe.wait_ge(s["f_sb"], j)
                to_nat(fo[:, b, :], G1).then_inc(s["f_ps"], 1)

            def out_unit(i, b):
                j = i * 2 + b
                if again(i):
                    pe.wait_ge(s["f_g"], j - 1)
                else:
                    pe.wait_ge(s["mrg_a" if b == 0 else "mrg"], KT)
                for n in range(8):
                    if not again(i) and b == 0:
                        pe.wait_ge(s["m_lo"], 2 * n + 2)
                    products(i * 8 + SPLIT_OUT, 4 * b + n // 2, n % 2, Hh, Hl, 2 * n, b, n == 0, n == 7)
                    if n == 1 and (again(i) or b):
                        out_turn(j - 1, 1 - b)
            out_unit(0, 0)
            out_unit(0, 1)
            with pe.Fori(1, KT // 2) as i:
                out_unit(i, 0)
                out_unit(i, 1)
            out_turn(KT - 1, 1)


ACT_LINKS = 3
DVE_LINKS = 63

_INS = ["x_prompt", "x_sample", "c_prompt", "c_sample", "state_conv", "state_delta", "cache_k", "cache_v", "norm_w", "ada_w",
        "ada_b", "w_in", "conv_w", "gdn_a_log", "gdn_dt_bias", "gdn_norm_w", "q_norm_w", "k_norm_w", "rel_bias", "w_proj_a",
        "w_proj_b", "w_out"]
_OUTS = {"y_prompt": (1, NP, D), "y_sample": (1, NS, D), "p_conv": (1, 1, 3, 3 * QK), "p_delta": (1, 1, HEADS, P, P),
         "p_k": (1, 1, NP, HEADS, P), "p_v": (1, 1, NP, HEADS, P), "s_conv": (1, 1, 3, 3 * QK),
         "s_delta": (1, 1, HEADS, P, P), "s_k": (1, 1, NS, HEADS, P), "s_v": (1, 1, NS, HEADS, P)}


def kernel(**inputs):
    import concourse.bacc as bacc
    from concourse.bass_utils import run_bass_kernel_spmd

    nc = bacc.Bacc("TRN2", target_bir_lowering=False, num_devices=1)
    arrays = {n: np.ascontiguousarray(inputs[n]) for n in _INS}
    rel = arrays.pop("rel_bias")[0]
    arrays["rel_ext"] = np.ascontiguousarray(np.concatenate([rel[:, 1:], np.repeat(rel[:, -1:], P - 1, axis=1)], axis=1))
    arrays["con"] = constants()
    io = {n: nc.dram_tensor(f"in_{n}", a.shape, mybir.dt.from_np(a.dtype), kind="ExternalInput").ap() for n, a in arrays.items()}
    for n, shape in _OUTS.items():
        io[n] = nc.dram_tensor(f"out_{n}", shape, F32, kind="ExternalOutput").ap()
    hybrid_layer(nc, io)
    r = run_bass_kernel_spmd(nc, [{f"in_{n}": a for n, a in arrays.items()}], core_ids=[0])
    return tuple(r.results[0][f"out_{n}"] for n in _OUTS)
```
